# Optimizing a Trainium2 kernel written in Bass

```python
import math
import jax
import jax.numpy as jnp
from jax import lax
import numpy as np

D_MODEL = 1024
BATCH = 1
SEQ = 256
DEPTH = 1

D_MIX = D_MODEL
CONV_WIDTH = D_MIX // 2
CONV_GROUPS = 8
CONV_K = 3
GLA_WIDTH = D_MIX - CONV_WIDTH
GLA_HEADS = 4
GLA_DV = GLA_WIDTH // GLA_HEADS
GLA_DK = GLA_DV // 2
GLA_RANK = 16
GLA_NORMALIZER = 16.0
GLA_CHUNK = 64
N_EXPERTS = 32
TOP_K = 4
D_FF = D_MODEL
SWIGLU_LIMIT = 7.0
SWIGLU_ALPHA = 1.702
MOE_BLOCK = 256
RMS_EPS = 1e-5
D_IN = 3 * CONV_WIDTH + 2 * GLA_HEADS * GLA_DK + 2 * GLA_WIDTH + GLA_RANK

kernel_name = "hybrid_conv_gla_moe_block"

def rmsnorm(x, g):
    xf = x.astype(jnp.float32)
    y = xf * lax.rsqrt(jnp.mean(xf * xf, axis=-1, keepdims=True) + RMS_EPS)
    return (y * g.astype(jnp.float32)).astype(x.dtype)

def gla_chunked(q, k, v, log_a):
    bsz, nh, s, dk = q.shape
    dv = v.shape[-1]
    n = s // GLA_CHUNK
    q = q.reshape(bsz, nh, n, GLA_CHUNK, dk)
    k = k.reshape(bsz, nh, n, GLA_CHUNK, dk)
    v = v.reshape(bsz, nh, n, GLA_CHUNK, dv)
    b = jnp.cumsum(log_a.reshape(bsz, nh, n, GLA_CHUNK, dk), axis=3)
    b_last = b[..., -1:, :]
    q_dec = q * jnp.exp(b)
    k_dec = k * jnp.exp(-b)
    mask = jnp.tril(jnp.ones((GLA_CHUNK, GLA_CHUNK), dtype=bool))
    scores = jnp.where(mask, jnp.einsum('bhncd,bhnjd->bhncj', q_dec, k_dec), 0.0)
    o_intra = jnp.einsum('bhncj,bhnjv->bhncv', scores, v)
    kv = jnp.einsum('bhncd,bhncv->bhndv', k * jnp.exp(b_last - b), v)
    decay = jnp.exp(b_last[..., 0, :])

    def step(state, inp):
        dec, kv_n = inp
        return dec[..., None] * state + kv_n, state

    init = jnp.zeros((bsz, nh, dk, dv), q.dtype)
    _, s_before = lax.scan(step, init, (jnp.moveaxis(decay, 2, 0), jnp.moveaxis(kv, 2, 0)))
    s_before = jnp.moveaxis(s_before, 0, 2)
    o_inter = jnp.einsum('bhncd,bhndv->bhncv', q_dec, s_before)
    return (o_intra + o_inter).reshape(bsz, nh, s, dv)

def hybrid_mixer(h, w_in, conv_w, w_gk_up, b_gk_up, gla_norm_g, w_out):
    bsz, s, _ = h.shape
    sizes = [CONV_WIDTH, CONV_WIDTH, CONV_WIDTH, GLA_HEADS * GLA_DK, GLA_HEADS * GLA_DK,
             GLA_WIDTH, GLA_WIDTH, GLA_RANK]
    splits = [int(v) for v in np.cumsum(sizes)[:-1]]
    proj = h @ w_in
    u_h, gate_b, gate_c, q, k, v, g_out, gk_low = jnp.split(proj, splits, axis=-1)

    u = gate_c * u_h
    u_pad = jnp.pad(u, ((0, 0), (CONV_K - 1, 0), (0, 0)))
    conv = conv_w[0] * u_pad[:, 0:s]
    for i in range(1, CONV_K):
        conv = conv + conv_w[i] * u_pad[:, i:i + s]
    y_conv = gate_b * conv

    gk = gk_low @ w_gk_up + b_gk_up
    log_a = jax.nn.log_sigmoid(gk.astype(jnp.float32)) / GLA_NORMALIZER

    def heads(t, d):
        return t.astype(jnp.float32).reshape(bsz, s, GLA_HEADS, d).transpose(0, 2, 1, 3)

    o = gla_chunked(heads(q, GLA_DK) * (GLA_DK ** -0.5), heads(k, GLA_DK),
                    heads(v, GLA_DV), heads(log_a, GLA_DK))
    o = rmsnorm(o, gla_norm_g)
    o = o.transpose(0, 2, 1, 3).reshape(bsz, s, GLA_WIDTH).astype(h.dtype)
    y_gla = o * jax.nn.silu(g_out)

    return jnp.concatenate([y_conv, y_gla], axis=-1) @ w_out

def moe(h, w_router, b_router, w_gate_up, b_gate_up, w_down, b_down):
    bsz, s, d = h.shape
    t = bsz * s
    xf = h.reshape(t, d)
    logits = (xf @ w_router + b_router).astype(jnp.float32)
    top_v, top_i = lax.top_k(logits, TOP_K)
    gates = jax.nn.softmax(top_v, axis=-1).astype(h.dtype)

    tk = t * TOP_K
    e_flat = top_i.reshape(tk).astype(jnp.int32)
    tok_flat = jnp.repeat(jnp.arange(t, dtype=jnp.int32), TOP_K)
    gate_flat = gates.reshape(tk)

    counts = jnp.zeros((N_EXPERTS,), jnp.int32).at[e_flat].add(1)
    padded = ((counts + MOE_BLOCK - 1) // MOE_BLOCK) * MOE_BLOCK
    pad_end = jnp.cumsum(padded)
    pad_start = pad_end - padded
    grp_start = jnp.cumsum(counts) - counts
    order = jnp.argsort(e_flat, stable=True)
    e_sorted = e_flat[order]
    dest = pad_start[e_sorted] + (jnp.arange(tk, dtype=jnp.int32) - grp_start[e_sorted])

    n_rows = (-(-tk // MOE_BLOCK)) * MOE_BLOCK + N_EXPERTS * MOE_BLOCK
    n_blocks = n_rows // MOE_BLOCK
    row_tok = jnp.full((n_rows,), t, jnp.int32).at[dest].set(tok_flat[order])
    row_gate = jnp.zeros((n_rows,), h.dtype).at[dest].set(gate_flat[order])
    block_expert = jnp.minimum(
        jnp.searchsorted(pad_end, jnp.arange(n_blocks, dtype=jnp.int32) * MOE_BLOCK, side='right'),
        N_EXPERTS - 1).astype(jnp.int32)

    x_pad = jnp.concatenate([xf, jnp.zeros((1, d), xf.dtype)], axis=0)
    x_blocks = x_pad[row_tok].reshape(n_blocks, MOE_BLOCK, d)

    def expert_block(args):
        xb, eid = args
        gu = xb @ w_gate_up[eid] + b_gate_up[eid]
        gate = jnp.minimum(gu[:, :D_FF], SWIGLU_LIMIT)
        up = jnp.clip(gu[:, D_FF:], -SWIGLU_LIMIT, SWIGLU_LIMIT)
        glu = gate * jax.nn.sigmoid(gate * SWIGLU_ALPHA)
        return ((up + 1.0) * glu) @ w_down[eid] + b_down[eid]

    out = lax.map(expert_block, (x_blocks, block_expert)).reshape(n_rows, d)
    y = jnp.zeros((t + 1, d), h.dtype).at[row_tok].add(out * row_gate[:, None])[:t]
    return y.reshape(bsz, s, d)

def setup_inputs(seed: int = 0) -> dict:
    key = jax.random.key(seed)
    ks = jax.random.split(key, 17)
    f32 = jnp.float32

    def nrm(k, shape, scale):
        return jax.random.normal(k, shape, f32) * scale

    return {
        "x": nrm(ks[0], (BATCH, SEQ, D_MODEL), 1.0),
        "norm_mix_g": 1.0 + nrm(ks[1], (DEPTH, D_MODEL), 0.02),
        "w_in": nrm(ks[2], (DEPTH, D_MODEL, D_IN), D_MODEL ** -0.5),
        "conv_w": nrm(ks[3], (DEPTH, CONV_K, CONV_WIDTH), CONV_K ** -0.5),
        "w_gk_up": nrm(ks[4], (DEPTH, GLA_RANK, GLA_HEADS * GLA_DK), GLA_RANK ** -0.5),
        "b_gk_up": nrm(ks[5], (DEPTH, GLA_HEADS * GLA_DK), 0.1),
        "gla_norm_g": 1.0 + nrm(ks[6], (DEPTH, GLA_DV), 0.02),
        "w_out": nrm(ks[7], (DEPTH, D_MIX, D_MODEL), D_MIX ** -0.5),
        "norm_ffn_g": 1.0 + nrm(ks[8], (DEPTH, D_MODEL), 0.02),
        "w_router": nrm(ks[9], (DEPTH, D_MODEL, N_EXPERTS), D_MODEL ** -0.5),
        "b_router": nrm(ks[10], (DEPTH, N_EXPERTS), 0.01),
        "w_gate_up": nrm(ks[11], (DEPTH, N_EXPERTS, D_MODEL, 2 * D_FF), D_MODEL ** -0.5),
        "b_gate_up": nrm(ks[12], (DEPTH, N_EXPERTS, 2 * D_FF), 0.02),
        "w_down": nrm(ks[13], (DEPTH, N_EXPERTS, D_FF, D_MODEL), D_FF ** -0.5),
        "b_down": nrm(ks[14], (DEPTH, N_EXPERTS, D_MODEL), 0.02),
        "norm_final_g": 1.0 + nrm(ks[15], (D_MODEL,), 0.02),
    }

def reference(x, norm_mix_g, w_in, conv_w, w_gk_up, b_gk_up, gla_norm_g, w_out,
              norm_ffn_g, w_router, b_router, w_gate_up, b_gate_up, w_down, b_down,
              norm_final_g):
    for l in range(DEPTH):
        h = rmsnorm(x, norm_mix_g[l])
        x = x + hybrid_mixer(h, w_in[l], conv_w[l], w_gk_up[l], b_gk_up[l],
                             gla_norm_g[l], w_out[l])
        h = rmsnorm(x, norm_ffn_g[l])
        x = x + moe(h, w_router[l], b_router[l], w_gate_up[l], b_gate_up[l],
                    w_down[l], b_down[l])
    return rmsnorm(x, norm_final_g)


_drawn_inputs = setup_inputs


def setup_inputs(seed=0):
    import zlib

    import numpy as np

    out = dict(_drawn_inputs(seed))
    spreads = {}
    factors = {'gla_norm_g': 3.248,
     'b_router': 2.917,
     'b_gate_up': 6.225,
     'b_down': 7.204,
     'norm_final_g': 2.868}
    for name, (base, spread) in spreads.items():
        noise = np.random.default_rng([zlib.crc32(name.encode()), seed]).standard_normal(out[name].shape)
        drawn = base * np.exp(spread * noise) if base else spread * noise
        out[name] = jnp.asarray(drawn.astype(out[name].dtype))
    for name, factor in factors.items():
        out[name] = (out[name] * factor).astype(out[name].dtype)
    return out
```

```python
import numpy as np
import concourse.bass as bass
from concourse import mybir
from contextlib import ExitStack

P = 128
D = 1024
T = 256
TT = T // P
KT = D // P
CONV = 512
CT = CONV // P
TAPS = 3
HEADS = 4
DK = 64
DV = 128
PAIRS = HEADS // 2
CH = 64
NCH = T // CH
RANK = 16
NORMALIZER = 16.0
E = 32
TOP = 4
F = 1024
LIMIT = 7.0
ALPHA = 1.702
EPS = 1e-5
SLOTS = 64
BLOCKS = T // SLOTS
EXTRA = T * TOP // SLOTS
TABLE = E + 2 * EXTRA
NCOLS = 2 + 1 + TAPS * CT

CHUNK = 4096
RING = 6
MIX_CHUNKS = 8
QK, VV, GG, UU, CC, BB, WO = range(7)
ITEM_CHUNKS = 6
UNIT = 1024
UNITS = ITEM_CHUNKS * CHUNK // UNIT
WHOLE = (0, 1, 16, 17)
SPLIT = [u for u in range(UNITS) if u not in WHOLE]
BUFS = 4
assert len(SPLIT) % BUFS == 0
FREED = [u for u in SPLIT if u % 4 != 3]
AHEAD = sum(u % 4 != 3 for u in SPLIT[-BUFS:])


def slot_of(chunk):
    return chunk % RING


def build(nc, x, norm_mix_g, w_in, conv_w, w_gk_up, b_gk_up, gla_norm_g, w_out, norm_ffn_g,
          w_router, b_router, w_gate_up, b_gate_up, w_down, b_down, norm_final_g, out):
    f32 = mybir.dt.float32
    f32r = mybir.dt.float32r
    i32 = mybir.dt.int32
    ALU = mybir.AluOpType
    ACT = mybir.ActivationFunctionType
    AX = mybir.AxisListType
    ds = bass.ds

    x_v = x[0].rearrange("(t p) d -> p t d", p=P)
    out_v = out[0].rearrange("(t p) d -> p t d", p=P)
    win_v = w_in[0].rearrange("(k p) n -> p k n", p=P)
    wout_v = w_out[0].rearrange("(k p) n -> p k n", p=P)
    wr_v = w_router[0].rearrange("(k p) n -> p k n", p=P)
    gu_v = w_gate_up[0].rearrange("e (k p) n -> p e k n", p=P)
    dn_v = w_down[0].rearrange("e (k p) n -> p e k n", p=P)
    col0 = {UU: 0, BB: CONV, CC: 2 * CONV, QK: 3 * CONV, VV: 4 * CONV, GG: 5 * CONV}
    GKLOW0 = 6 * CONV

    ctx = ExitStack()
    with ctx:
        def sb(name, shape, dt=f32, scope=ctx):
            return scope.enter_context(nc.sbuf_tensor(name, shape, dt))

        def sem(name):
            return ctx.enter_context(nc.semaphore(name))

        ring = sb("ring", [P, RING, CHUNK])
        xs = sb("x_sb", [P, TT, D])
        g_bc = sb("g_bc", [P, D])
        ident = sb("ident", [P, P])
        ones = sb("ones", [P, P])
        before = sb("before", [P, P])
        fold = sb("fold", [P, SLOTS])
        slot1 = sb("slot1", [P, BLOCKS, P])
        eps_c = sb("eps_c", [P, 1])
        one_c = sb("one_c", [P, 1])
        ss = sb("ss", [P, TT])
        var = sb("var", [P, TT])
        lnv = sb("lnv", [P, TT])
        rstd = sb("rstd", [P, TT])
        tmp2 = sb("tmp2", [P, TT])
        gates = sb("gates", [P, TT, E])
        rank1 = sb("rank1", [P, TT, E])
        bias_t = sb("bias_t", [P, 2, F // P, E])
        bias_e = sb("bias_e", [P, 2, F // P])
        table = sb("table", [1, 2 * TABLE], i32)
        n_items = sb("n_items", [1, 1], i32)

        router = ExitStack()
        mixer = ExitStack()
        late = ExitStack()

        def rb(name, shape, dt=f32):
            return sb(name, shape, dt, router)

        h_t = rb("h_t", [P, KT, T])
        h_row = rb("h_row", [P, TT, D])
        y_t = h_row[:, :, :].rearrange("p t (k n) -> p (t k) n", n=T)
        gffn_bc = rb("gffn_bc", [P, D])
        wr = rb("wr", [P, KT, E])
        br_bc = rb("br_bc", [P, E])
        lg = rb("lg", [P, TT, E])
        lmax = rb("lmax", [P, TT, 8])
        ngt = rb("ngt", [P, TT])
        gt = rb("gt", [P, TT, E])
        eq = rb("eq", [P, TT, E])
        cum = rb("cum", [P, TT, E])
        chosen = rb("chosen", [P, TT, E])
        ex = rb("ex", [P, TT, E])
        gates_t = rb("gates_t", [E, TT, P])
        cnt = rb("cnt", [E, 1])
        more = rb("more", [E, BLOCKS - 1])
        block_c = rb("block_c", [E, BLOCKS - 1])
        boff_c = rb("boff_c", [E, BLOCKS - 1])
        exp_c = rb("exp_c", [E, 1])
        place = rb("place", [E, BLOCKS - 1])
        extra1 = rb("extra1", [E, EXTRA])
        hot = rb("hot", [E, BLOCKS - 1, EXTRA])
        table_f = rb("table_f", [1, 2 * TABLE])
        n_f = rb("n_f", [1, BLOCKS - 1])

        def mb(name, shape, dt=f32):
            return sb(name, shape, dt, mixer)

        wgk = mb("wgk", [P, KT, RANK])
        wgu = mb("wgu", [RANK, PAIRS, P])
        rows = mb("rows", [NCOLS, P])
        cols = mb("cols", [P, NCOLS])
        gkl = mb("gkl", [RANK, T])
        gk = mb("gk", [P, PAIRS, T])
        la = mb("la", [P, PAIRS, T])
        lb = mb("lb", [P, PAIRS, T])
        e_pos = mb("e_pos", [P, PAIRS, T])
        e_neg = mb("e_neg", [P, PAIRS, T])
        e_rem = mb("e_rem", [P, PAIRS, T])
        qk = mb("qk", [P, 2, PAIRS, T])
        o_r = qk[:, :, :, :].rearrange("p a b t -> p (a b) t")
        q_dec = mb("q_dec", [P, PAIRS, T])
        k_dec = mb("k_dec", [P, PAIRS, 2, T])
        o_sq = k_dec[:, :, :, :].rearrange("p a b t -> p (a b) t")
        k_rem = mb("k_rem", [P, PAIRS, T])
        k_row = mb("k_row", [P, TT, PAIRS * P])
        v_row = mb("v_row", [P, TT, HEADS * DV])
        g_t = mb("g_t", [P, HEADS, T])
        sil = mb("sil", [P, HEADS, T])
        state = mb("state", [P, NCH - 1, PAIRS, 2, DV])
        sc = mb("sc", [P, TT, HEADS, P])
        reset = mb("reset", [P, PAIRS * NCH, CH])
        u_t = mb("u_t", [P, CT, T])
        u_pad = mb("u_pad", [P, CT, T + TAPS - 1])
        conv = mb("conv", [P, CT, T])
        mixer.close()

        bgu = sb("bgu", [E, 2 * F], f32, late)
        bdn = sb("bdn", [E, D], f32, late)
        late.close()
        router.close()

        w_hi = sb("w_hi", [P, BUFS, UNIT], f32r)
        w_lo = sb("w_lo", [P, BUFS, UNIT], f32r)
        z_hi = sb("z_hi", [P, D], f32r)
        z_lo = sb("z_lo", [P, D], f32r)
        h2_hi = sb("h2_hi", [P, TT, D], f32r)
        h2_lo = sb("h2_lo", [P, TT, D], f32r)
        x_sp = sb("x_sp", [P, KT, 2, SLOTS], f32r)
        p_row = sb("p_row", [P, TT, P], f32r)
        gate_c = sb("gate_c", [P, TT])
        up_sb = sb("up_sb", [P, 2, 512])
        gu_b = sb("gu_b", [P, 2, 4, SLOTS])
        g_lim = sb("g_lim", [P, 4, SLOTS])
        u_lim = sb("u_lim", [P, 4, SLOTS])
        g_exp = sb("g_exp", [P, 4, SLOTS])
        act = sb("act", [P, 4, SLOTS])
        a_sp = sb("a_sp", [P, F // P, 2, SLOTS], f32r)
        p_t = sb("p_t", [P, T], f32r)
        gate_s = sb("gate_s", [P, 1])
        y_out = sb("y_out", [P, TT, D])

        bank = [ctx.enter_context(nc.psum_tensor(f"bank{i}", [P, 512], f32)) for i in range(8)]
        y_ps = [[bank[4 + 2 * t + n] for n in range(2)] for t in range(TT)]

        s_x = sem("x_loaded")
        s_gmix = sem("g_mix_loaded")
        s_small = sem("small_loaded")
        s_late = sem("router_weights_loaded")
        s_bias = sem("expert_biases_loaded")
        s_gfin = sem("g_final_loaded")
        s_slot = [sem(f"slot{i}_loaded") for i in range(RING)]
        s_used = sem("chunk_used")
        s_const = sem("consts_ready")
        s_ss = sem("squares_summed")
        s_var = sem("variance_ready")
        s_rs = sem("rsqrt_ready")
        s_h = sem("h_ready")
        s_tr = sem("transposed")
        s_trA = sem("transposed_kept_act")
        s_trD = sem("transposed_kept_dve")
        s_small_t = sem("small_transposed")
        s_cols = sem("cols_ready")
        s_pj = sem("projected")
        s_pk = sem("projection_kept")
        s_gk = sem("gk_ready")
        s_gkb = sem("gk_biased")
        s_ln = sem("softplus_ready")
        s_cs = sem("log_sums_ready")
        s_ex = sem("decays_ready")
        s_dec = sem("decayed_ready")
        s_kt = sem("k_transposed")
        s_krow = sem("k_row_ready")
        s_kv = sem("kv_ready")
        s_st = sem("state_ready")
        s_sc = sem("scores_ready")
        s_sck = sem("scores_kept")
        s_mask = sem("scores_masked")
        s_o = sem("o_ready")
        s_osq = sem("o_squared")
        s_ms = sem("o_mean_ready")
        s_or = sem("o_rsqrt_ready")
        s_sg = sem("silu_exp_ready")
        s_ygla = sem("y_gla_ready")
        s_yconv = sem("y_conv_ready")
        s_op = sem("out_projected")
        s_x2 = sem("x2_ready")
        s_h2 = sem("h2_ready")
        s_h2hi = sem("h2_hi_ready")
        s_h2lo = sem("h2_lo_ready")
        s_bt = sem("bias_transposed")
        s_btk = sem("bias_t_ready")
        s_lg = sem("logits_ready")
        s_lgk = sem("logits_less_max")
        s_le = sem("logits_exp")
        s_cho = sem("chosen_ready")
        s_cnt = sem("counted")
        s_more = sem("more_ready")
        s_pref = sem("prefix_ready")
        s_hot = sem("hot_ready")
        s_tab = sem("table_summed")
        s_items = sem("items_ready")
        s_gt = sem("gates_transposed")
        s_gtk = sem("gates_t_ready")
        s_mixed = sem("mixer_space_free")
        s_free = sem("split_buffer_free")
        s_hi = sem("w_hi_ready")
        s_lo = sem("w_lo_ready")
        s_p = sem("p_row_ready")
        s_xg = sem("x_gathered")
        s_xs = sem("x_split_ready")
        s_pt = sem("p_transposed")
        s_ptk = sem("p_t_ready")
        s_up = sem("up_kept")
        s_gu = sem("gate_up_folded")
        s_gur = sem("gate_up_read")
        s_ge = sem("gate_exp_ready")
        s_gl = sem("gate_limited")
        s_a = sem("activation_ready")
        s_dn = sem("down_first_ready")
        s_zh = sem("z_hi_ready")
        s_zl = sem("z_lo_ready")
        s_y = sem("item_added")
        s_x3 = sem("x3_ready")
        s_last = sem("last_norm_step")
        s_fin = sem("out_ready")
        s_out = sem("out_stored")
        s_dve = sem("dve_step")
        s_pool = sem("pool_step")
        s_act = sem("act_step")

        PROJ = [(QK, 0), (QK, 1), ("gk", 0), (VV, 0), (VV, 1), (GG, 0), (GG, 1),
                (UU, 0), (UU, 1), (CC, 0), (CC, 1), (BB, 0), (BB, 1)]
        OUT_BANK = (5, 6, 1, 2)

        def two_tiles(n):
            return bank[n % 4][:, :].rearrange("p (a t) -> p a t", a=2)

        def chunk_view(c, k):
            return ring[:, slot_of(c), :].rearrange("p (k n) -> p k n", k=k)

        def item_slot(j):
            return slot_of(MIX_CHUNKS + j)

        def item_loaded(it, j):
            return (it + (MIX_CHUNKS + j) // RING + 1) * 16

        block = ctx.enter_context(nc.Block())

        @block.sync
        def _(sp):
            sp.dma_start(xs[:, :, :], x_v).then_inc(s_x, 16)
            for c in range(MIX_CHUNKS):
                if c >= RING:
                    sp.wait_ge(s_used, c - RING + 1)
                if c < WO:
                    src = win_v[:, :, col0[c]:col0[c] + 512]
                else:
                    src = wout_v[:, :, (c - WO) * 512:(c - WO + 1) * 512]
                sp.dma_start(chunk_view(c, KT), src).then_inc(s_slot[slot_of(c)], 16)

            def load_item(it, e):
                for j in range(ITEM_CHUNKS):
                    sp.wait_ge(s_used, it * ITEM_CHUNKS + (MIX_CHUNKS + j - RING + 1))
                    if j < 4:
                        c0 = (j % 2) * F + (j // 2) * 512
                        src = gu_v[:, ds(e, 1), :, c0:c0 + 512].rearrange("p e k n -> p (e k) n")
                        dst = ring[:, item_slot(j), :].rearrange("p (k n) -> p k n", k=KT)
                    else:
                        src = dn_v[:, ds(e, 1), 4 * (j - 4):4 * (j - 3), :].rearrange("p e k n -> p (e k) n")
                        dst = ring[:, item_slot(j), :].rearrange("p (k n) -> p k n", k=4)
                    sp.dma_start(dst, src).then_inc(s_slot[item_slot(j)], 16)

            with sp.Fori(0, E) as it:
                load_item(it, it)
            sp.wait_ge(s_items, 1)
            n = sp.value_load(n_items[0:1, 0:1], min_val=E, max_val=E + EXTRA)
            with sp.If(n > E):
                with sp.Fori(E, n) as it:
                    e = sp.value_load(table[0:1, ds(it, 1)], min_val=0, max_val=E - 1)
                    load_item(it, e)
            for t in range(TT):
                sp.wait_ge(s_fin, t + 1)
                sp.dma_start(out_v[:, t, :], y_out[:, t, :]).then_inc(s_out, 16)
            sp.wait_ge(s_out, 16 * TT)

        @block.gpsimd
        def _(pool):
            steps = [0]

            def link(ins):
                steps[0] += 1
                ins.then_inc(s_pool, 1)
                pool.wait_ge(s_pool, steps[0])

            link(pool.memset(ident[:, :], 0.0))
            link(pool.affine_select(out=ident[:, :], in_=ident[:, :], compare_op=ALU.not_equal, fill=1.0,
                                    base=0, pattern=[[-1, P]], channel_multiplier=1))
            link(pool.memset(ones[:, :], 1.0))
            link(pool.memset(eps_c[:, :], EPS))
            pool.memset(one_c[:, :], 1.0).then_inc(s_const, 1)
            link(pool.memset(k_dec[:, :, :, :], 0.0))
            link(pool.memset(u_pad[:, :, 0:TAPS - 1], 0.0))
            link(pool.memset(state[:, :, :, :, :], 0.0))
            link(pool.memset(sc[:, :, :, :], 0.0))
            link(pool.memset(reset[:, :, :], 1.0))
            pool.affine_select(out=reset[:, :, :], in_=reset[:, :, :], compare_op=ALU.is_gt, fill=0.0,
                               base=0, pattern=[[0, PAIRS * NCH], [1, CH]], channel_multiplier=0).then_inc(s_const, 1)
            link(pool.affine_select(out=before[:, :], in_=ones[:, :], compare_op=ALU.is_gt, fill=0.0,
                                    base=0, pattern=[[1, P]], channel_multiplier=-1))
            link(pool.memset(fold[:, :], 0.0))
            for off in (0, SLOTS):
                link(pool.affine_select(out=fold[:, :], in_=fold[:, :], compare_op=ALU.not_equal, fill=1.0,
                                        base=-off, pattern=[[-1, SLOTS]], channel_multiplier=1))
            link(pool.iota(slot1[:, :, :], pattern=[[SLOTS, BLOCKS], [0, 2], [1, SLOTS]], base=1,
                           channel_multiplier=0, allow_small_or_imprecise_dtypes=True))
            link(pool.iota(block_c[:, :], pattern=[[SLOTS, BLOCKS - 1]], base=SLOTS,
                           channel_multiplier=0, allow_small_or_imprecise_dtypes=True))
            link(pool.iota(boff_c[:, :], pattern=[[P, BLOCKS - 1]], base=P,
                           channel_multiplier=0, allow_small_or_imprecise_dtypes=True))
            link(pool.iota(exp_c[:, :], pattern=[[0, 1]], base=0,
                           channel_multiplier=1, allow_small_or_imprecise_dtypes=True))
            link(pool.iota(extra1[:, :], pattern=[[1, EXTRA]], base=1,
                           channel_multiplier=0, allow_small_or_imprecise_dtypes=True))
            link(pool.memset(table_f[:, :], 0.0))
            pool.iota(table_f[:, 0:E], pattern=[[1, E]], base=0,
                      channel_multiplier=0, allow_small_or_imprecise_dtypes=True).then_inc(s_const, 1)
            for t in range(TT):
                pool.wait_ge(s_sck, 2 * (t + 1))
                pool.affine_select(out=sc[:, t, :, :], in_=sc[:, t, :, :], compare_op=ALU.is_ge, fill=0.0,
                                   base=0, pattern=[[0, HEADS], [1, P]], channel_multiplier=-1).then_inc(s_mask, 1)

        @block.scalar
        def _(act_e):
            steps = [0]

            def link(ins):
                steps[0] += 1
                ins.then_inc(s_act, 1)
                act_e.wait_ge(s_act, steps[0])

            act_e.dma_start(g_bc[:, :], norm_mix_g.partition_broadcast(P)[:, 0, :]).then_inc(s_gmix, 16)
            act_e.dma_start(rows[0:2, :], b_gk_up[0].rearrange("(a p) -> a p", p=P)).then_inc(s_small, 16)
            act_e.dma_start(rows[2:3, :], gla_norm_g).then_inc(s_small, 16)
            for i in range(TAPS):
                act_e.dma_start(rows[3 + i * CT:3 + (i + 1) * CT, :],
                                conv_w[0, i].rearrange("(a p) -> a p", p=P)).then_inc(s_small, 16)
            act_e.dma_start(wgk[:, :, :], win_v[:, :, GKLOW0:GKLOW0 + RANK]).then_inc(s_small, 16)
            act_e.dma_start(wgu[:, :, :], w_gk_up[0].rearrange("r (a p) -> r a p", p=P)).then_inc(s_small, 16)
            act_e.dma_start(gffn_bc[:, :], norm_ffn_g.partition_broadcast(P)[:, 0, :]).then_inc(s_late, 16)
            act_e.dma_start(wr[:, :, :], wr_v).then_inc(s_late, 16)
            act_e.dma_start(br_bc[:, :], b_router.partition_broadcast(P)[:, 0, :]).then_inc(s_late, 16)

            act_e.wait_ge(s_const, 1)

            def squares(junk):
                for t in range(TT):
                    act_e.activation(junk[:, t, :], xs[:, t, :], ACT.Square,
                                     accum_out=ss[:, t:t + 1]).then_inc(s_ss, 1)

            def rsqrt(n):
                act_e.wait_ge(s_var, n)
                link(act_e.activation(lnv[:, :], var[:, :], ACT.Ln))
                act_e.activation(rstd[:, :], lnv[:, :], ACT.Exp, scale=-0.5).then_inc(s_rs, 1)

            act_e.wait_ge(s_x, 16)
            squares(h_row)
            rsqrt(1)
            for i in (0, 2):
                act_e.wait_ge(s_tr, i + 1)
                act_e.copy(h_t[:, 2 * i:2 * i + 2, :], bank[i][:, :].rearrange("p (a t) -> p a t", a=2)).then_inc(s_trA, 1)

            def keep(n):
                what, i = PROJ[n]
                src = bank[n % 4]
                two = src[:, :].rearrange("p (a t) -> p a t", a=2)
                act_e.wait_ge(s_pj, n + 1)
                if what == "gk":
                    o, src_ap = gkl[:, :], src[0:RANK, 0:T]
                elif what == VV:
                    o, src_ap = v_row[:, i, :], src[:, :]
                elif what == QK:
                    o, src_ap = qk[:, i, :, :], two
                else:
                    o, src_ap = {GG: g_t, UU: u_t}[what][:, 2 * i:2 * i + 2, :], two
                act_e.copy(o, src_ap).then_inc(s_pk, 1)

            for n in range(3):
                keep(n)
            act_e.wait_ge(s_gkb, 1)
            link(act_e.activation(la[:, :, :], gk[:, :, :], ACT.Abs))
            link(act_e.activation(lb[:, :, :], la[:, :, :], ACT.Exp, scale=-1.0))
            act_e.activation(la[:, :, :], lb[:, :, :], ACT.Ln, bias=one_c[:, 0:1]).then_inc(s_ln, 1)
            keep(3)
            act_e.wait_ge(s_cs, 1)
            act_e.activation(e_pos[:, :, :], lb[:, :, :], ACT.Exp, scale=1.0 / NORMALIZER).then_inc(s_ex, 1)
            act_e.activation(e_neg[:, :, :], lb[:, :, :], ACT.Exp, scale=-1.0 / NORMALIZER).then_inc(s_ex, 1)
            act_e.activation(e_rem[:, :, :], gk[:, :, :], ACT.Exp, scale=1.0 / NORMALIZER).then_inc(s_ex, 1)
            for n in range(4, 7):
                keep(n)
            act_e.wait_ge(s_pk, 7)
            act_e.activation(sil[:, :, :], g_t[:, :, :], ACT.Exp, scale=-1.0).then_inc(s_sg, 1)
            for n in range(7, 9):
                keep(n)
            for i in range(2):
                act_e.wait_ge(s_o, i + 1)
                act_e.activation(o_sq[:, 2 * i:2 * i + 2, :], bank[(7, 4)[i]][:, :].rearrange("p (a t) -> p a t", a=2),
                                 ACT.Square).then_inc(s_osq, 1)
            for i in range(2):
                act_e.wait_ge(s_ms, i + 1)
                o = o_r[:, 2 * i:2 * i + 2, :]
                link(act_e.activation(o, bank[5 + i][:, :].rearrange("p (a t) -> p a t", a=2), ACT.Ln,
                                      scale=1.0 / DV, bias=eps_c[:, 0:1]))
                act_e.activation(o, o, ACT.Exp, scale=-0.5).then_inc(s_or, 1)
            act_e.wait_ge(s_yconv, 2)
            act_e.dma_start(bgu[:, :], b_gate_up[0]).then_inc(s_bias, 16)
            act_e.dma_start(bdn[:, :], b_down[0]).then_inc(s_bias, 16)
            act_e.wait_ge(s_bt, 1)
            act_e.copy(bias_t[:, :, :, :].rearrange("p a f e -> p (a f e)"), bank[7][:, :]).then_inc(s_btk, 1)
            act_e.wait_ge(s_x2, 4)
            act_e.dma_start(g_bc[:, :], norm_final_g.rearrange("(a d) -> a d", a=1).partition_broadcast(P)[:, 0, :]).then_inc(s_gfin, 16)
            squares(h_row)
            rsqrt(2)
            for i in (0, 2):
                act_e.wait_ge(s_tr, 4 + i + 1)
                act_e.copy(h_t[:, 2 * i:2 * i + 2, :], bank[i][:, :].rearrange("p (a t) -> p a t", a=2)).then_inc(s_trA, 1)
            for t in range(TT):
                act_e.wait_ge(s_h2, t + 1)
                act_e.copy(h2_hi[:, t, :], h_row[:, t, :]).then_inc(s_h2hi, 1)
            act_e.wait_ge(s_lgk, 1)
            act_e.activation(ex[:, :, :], ex[:, :, :], ACT.Exp).then_inc(s_le, 1)
            act_e.wait_ge(s_le, 1)

            act_e.wait_ge(s_mixed, 2)
            act_e.wait_ge(s_items, 1)
            n = act_e.value_load(n_items[0:1, 0:1], min_val=E, max_val=E + EXTRA)

            def keep_gathered(it, half, src):
                act_e.wait_ge(s_xg, it * 2 + (half + 1))
                act_e.copy(x_sp[:, 4 * half:4 * half + 4, :, :].rearrange("p k a s -> p (k a s)"), src[:, :]).then_inc(s_xs, 1)

            keep_gathered(0, 0, bank[3])
            keep_gathered(0, 1, bank[0])

            with act_e.Fori(0, n) as it:
                def hi(u):
                    i = SPLIT.index(u)
                    j = u // 4
                    act_e.wait_ge(s_slot[item_slot(j)], item_loaded(it, j))
                    v = SPLIT[i - BUFS]
                    back = 0 if i >= BUFS else 1
                    if v % 4 == 3:
                        act_e.wait_ge(s_used, it * ITEM_CHUNKS + (MIX_CHUNKS + v // 4 + 1 - back * ITEM_CHUNKS))
                    else:
                        act_e.wait_ge(s_free, it * len(FREED) + (AHEAD + FREED.index(v) + 1 - back * len(FREED)))
                    act_e.copy(w_hi[:, i % BUFS, :], ring[:, item_slot(j), (u % 4) * UNIT:(u % 4 + 1) * UNIT]).then_inc(s_hi, 1)

                def keep_up(c):
                    act_e.wait_ge(s_used, it * ITEM_CHUNKS + (MIX_CHUNKS + c + 1))
                    act_e.wait_ge(s_gu, it * 4 + (c + 1))
                    act_e.copy(up_sb[:, c % 2, :], bank[c % 2][:, :]).then_inc(s_up, 1)

                def gate_exp(h):
                    act_e.wait_ge(s_gl, it * 2 + (h + 1))
                    act_e.activation(g_exp[:, :, :], g_lim[:, :, :], ACT.Exp, scale=-ALPHA).then_inc(s_ge, 1)

                for u in range(2, 7):
                    hi(u)
                act_e.wait_ge(s_pt, it + 1)
                act_e.copy(p_t[:, :], bank[3][:, 0:T])
                act_e.copy(gate_s[:, :], bank[3][:, T:T + 1]).then_inc(s_ptk, 1)
                keep_up(0)
                for u in range(7, 11):
                    hi(u)
                keep_up(1)
                for u in range(11, 14):
                    hi(u)
                gate_exp(0)
                hi(14)
                keep_up(2)
                hi(15)
                hi(18)
                keep_up(3)
                keep_gathered(it + 1, 0, bank[3])
                keep_gathered(it + 1, 1, bank[0])
                gate_exp(1)
                for u in range(19, 24):
                    hi(u)
                for i, nn in enumerate((1, 0)):
                    if i == 0:
                        act_e.wait_ge(s_dn, it + 1)
                    else:
                        act_e.wait_ge(s_used, it * ITEM_CHUNKS + (MIX_CHUNKS + ITEM_CHUNKS))
                        act_e.wait_ge(s_ptk, it + 1)
                    act_e.activation(z_hi[:, nn * 512:(nn + 1) * 512], bank[nn][:, :], ACT.Copy,
                                     scale=gate_s[:, 0:1]).then_inc(s_zh, 1)

            act_e.wait_ge(s_x3, 4)
            squares(y_out)
            rsqrt(3)

        @block.vector
        def _(dve):
            steps = [0]

            def link(ins):
                steps[0] += 1
                ins.then_inc(s_dve, 1)
                dve.wait_ge(s_dve, steps[0])

            def variance():
                link(dve.tensor_scalar(tmp2[:, :], ss[:, :], 1.0 / D, EPS, ALU.mult, ALU.add))
                dve.tensor_copy(var[:, :], tmp2[:, :]).then_inc(s_var, 1)

            def refine():
                link(dve.tensor_tensor(tmp2[:, :], rstd[:, :], rstd[:, :], ALU.mult))
                link(dve.tensor_tensor(tmp2[:, :], tmp2[:, :], var[:, :], ALU.mult))
                link(dve.tensor_scalar(tmp2[:, :], tmp2[:, :], -0.5, 1.5, ALU.mult, ALU.add))
                link(dve.tensor_tensor(rstd[:, :], rstd[:, :], tmp2[:, :], ALU.mult))

            dve.wait_ge(s_ss, 2)
            variance()
            dve.wait_ge(s_rs, 1)
            refine()
            dve.wait_ge(s_gmix, 16)
            for t in range(TT):
                dve.scalar_tensor_tensor(out=h_row[:, t, :], in0=xs[:, t, :], scalar=rstd[:, t:t + 1],
                                         in1=g_bc[:, :], op0=ALU.mult, op1=ALU.mult).then_inc(s_h, 1)
            dve.wait_ge(s_small_t, 1)
            link(dve.tensor_copy(cols[:, :], bank[4][:, 0:NCOLS]))
            for i in (1, 3):
                dve.wait_ge(s_tr, i + 1)
                dve.tensor_copy(h_t[:, 2 * i:2 * i + 2, :], bank[i][:, :].rearrange("p (a t) -> p a t", a=2)).then_inc(s_trD, 1)

            dve.wait_ge(s_gk, 1)
            for a in range(PAIRS):
                ins = dve.tensor_scalar(gk[:, a, :], bank[4][:, a * T:(a + 1) * T], cols[:, a:a + 1], None, ALU.add)
            ins.then_inc(s_gkb, 1)
            dve.wait_ge(s_const, 2)
            dve.wait_ge(s_ln, 1)
            link(dve.scalar_tensor_tensor(out=lb[:, :, :], in0=gk[:, :, :], scalar=0.0, in1=la[:, :, :],
                                          op0=ALU.min, op1=ALU.subtract))
            link(dve.tensor_copy(la[:, :, :], lb[:, :, :]))
            link(dve.tensor_tensor_scan(out=lb[:, :, :].rearrange("p a t -> p (a t)"),
                                        data0=reset[:, :, :].rearrange("p a t -> p (a t)"),
                                        data1=la[:, :, :].rearrange("p a t -> p (a t)"),
                                        initial=0.0, op0=ALU.mult, op1=ALU.add))
            lb_c = lb[:, :, :].rearrange("p a (n c) -> p (a n) c", c=CH)
            gk_c = gk[:, :, :].rearrange("p a (n c) -> p (a n) c", c=CH)
            dve.tensor_tensor(gk_c, lb_c[:, :, CH - 1:CH].broadcast_to([P, PAIRS * NCH, CH]), lb_c,
                              ALU.subtract).then_inc(s_cs, 1)
            dve.wait_ge(s_pk, 2)
            dve.wait_ge(s_ex, 1)
            dve.scalar_tensor_tensor(out=q_dec[:, :, :], in0=qk[:, 0, :, :], scalar=DK ** -0.5, in1=e_pos[:, :, :],
                                     op0=ALU.mult, op1=ALU.mult).then_inc(s_dec, 1)
            dve.wait_ge(s_ex, 2)
            for a in range(2):
                r = slice(DK * a, DK * (a + 1))
                dve.tensor_tensor(k_dec[r, :, a, :], qk[r, 1, :, :], e_neg[r, :, :], ALU.mult).then_inc(s_dec, 1)
            dve.wait_ge(s_ex, 3)
            dve.tensor_tensor(k_rem[:, :, :], qk[:, 1, :, :], e_rem[:, :, :], ALU.mult).then_inc(s_dec, 1)
            dve.wait_ge(s_kt, 1)
            dve.tensor_copy(k_row[:, :, :].rearrange("p t n -> p (t n)"), bank[5][:, :]).then_inc(s_krow, 1)

            def keep_scores(t):
                dve.wait_ge(s_sc, t + 1)
                src = bank[5 + t][:, :].rearrange("p (h c) -> p h c", h=HEADS)
                for a in range(2):
                    r = slice(CH * a, CH * (a + 1))
                    dve.tensor_copy(sc[r, t, :, r], src[r, :, r]).then_inc(s_sck, 1)

            for n in range(NCH - 1):
                dve.wait_ge(s_kv, n + 1)
                kv = bank[(6, 7, 4)[n]][:, :].rearrange("p (a b v) -> p a b v", a=PAIRS, b=2)
                for b in range(2):
                    r = slice(DK * b, DK * (b + 1))
                    if n == 0:
                        ins = dve.tensor_copy(state[r, 0, :, b, :], kv[r, :, b, :])
                    else:
                        for a in range(PAIRS):
                            last = (n + 1) * CH - 1
                            ins = dve.scalar_tensor_tensor(out=state[r, n, a, b, :], in0=state[r, n - 1, a, b, :],
                                                           scalar=e_pos[r, a, last:last + 1], in1=kv[r, a, b, :],
                                                           op0=ALU.mult, op1=ALU.add)
                ins.then_inc(s_st, 1)
                dve.wait_ge(s_st, n + 1)
            keep_scores(0)
            keep_scores(1)
            dve.wait_ge(s_sg, 1)
            link(dve.tensor_scalar(sil[:, :, :], sil[:, :, :], 1.0, None, ALU.add))
            link(dve.reciprocal(sil[:, :, :], sil[:, :, :]))
            link(dve.tensor_tensor(sil[:, :, :], sil[:, :, :], g_t[:, :, :], ALU.mult))
            link(dve.tensor_scalar(sil[:, :, :], sil[:, :, :], cols[:, 2:3], None, ALU.mult))

            for i in range(2):
                r = slice(2 * i, 2 * i + 2)
                dve.wait_ge(s_pk, 8 + i)
                dve.wait_ge(s_pj, 10 + i)
                link(dve.tensor_tensor(u_pad[:, r, TAPS - 1:], two_tiles(9 + i), u_t[:, r, :], ALU.mult))
                for j in range(TAPS):
                    for c in range(2 * i, 2 * i + 2):
                        w = cols[:, 3 + j * CT + c:4 + j * CT + c]
                        src = u_pad[:, c, j:j + T]
                        if j == 0:
                            ins = dve.tensor_scalar(conv[:, c, :], src, w, None, ALU.mult)
                        else:
                            ins = dve.scalar_tensor_tensor(out=conv[:, c, :], in0=src, scalar=w, in1=conv[:, c, :],
                                                           op0=ALU.mult, op1=ALU.add)
                    link(ins)
            for i in range(2):
                r = slice(2 * i, 2 * i + 2)
                dve.wait_ge(s_or, i + 1)
                link(dve.tensor_tensor(o_r[:, r, :], bank[(7, 4)[i]][:, :].rearrange("p (a t) -> p a t", a=2),
                                       o_r[:, r, :], ALU.mult))
                dve.tensor_tensor(y_t[:, CT + 2 * i:CT + 2 * i + 2, :], o_r[:, r, :], sil[:, r, :],
                                  ALU.mult).then_inc(s_ygla, 1)
            for i in range(2):
                r = slice(2 * i, 2 * i + 2)
                dve.wait_ge(s_pj, 12 + i)
                dve.tensor_tensor(y_t[:, r, :], two_tiles(11 + i), conv[:, r, :], ALU.mult).then_inc(s_yconv, 1)

            for n in range(2):
                for t in range(TT):
                    dve.wait_ge(s_op, 2 * n + t + 1)
                    dve.tensor_tensor(xs[:, t, n * 512:(n + 1) * 512], xs[:, t, n * 512:(n + 1) * 512],
                                      bank[OUT_BANK[2 * n + t]][:, :], ALU.add).then_inc(s_x2, 1)
            dve.wait_ge(s_ss, 4)
            variance()
            dve.wait_ge(s_rs, 2)
            refine()
            dve.wait_ge(s_late, 16 * 3)
            for t in range(TT):
                dve.scalar_tensor_tensor(out=h_row[:, t, :], in0=xs[:, t, :], scalar=rstd[:, t:t + 1],
                                         in1=gffn_bc[:, :], op0=ALU.mult, op1=ALU.mult).then_inc(s_h2, 1)
            for i in (1, 3):
                dve.wait_ge(s_tr, 4 + i + 1)
                dve.tensor_copy(h_t[:, 2 * i:2 * i + 2, :], bank[i][:, :].rearrange("p (a t) -> p a t", a=2)).then_inc(s_trD, 1)

            dve.wait_ge(s_lg, 1)
            link(dve.tensor_tensor(lg[:, :, :], bank[4][:, 0:TT * E].rearrange("p (t e) -> p t e", t=TT),
                                   br_bc[:, :].rearrange("p (a e) -> p a e", a=1).broadcast_to([P, TT, E]), ALU.add))
            for t in range(TT):
                ins = dve.max(out=lmax[:, t, :], in_=lg[:, t, :])
            link(ins)
            dve.tensor_tensor(ex[:, :, :], lg[:, :, :], lmax[:, :, 0:1].broadcast_to([P, TT, E]),
                              ALU.subtract).then_inc(s_lgk, 1)
            fourth = lmax[:, :, TOP - 1:TOP].broadcast_to([P, TT, E])
            dve.tensor_tensor(gt[:, :, :], lg[:, :, :], fourth, ALU.is_gt)
            link(dve.tensor_tensor(eq[:, :, :], lg[:, :, :], fourth, ALU.is_equal))
            dve.tensor_reduce(ngt[:, :], gt[:, :, :], AX.X, ALU.add)
            for t in range(TT):
                ins = dve.tensor_tensor_scan(out=cum[:, t, :], data0=ones[:, 0:E], data1=eq[:, t, :], initial=0.0,
                                             op0=ALU.mult, op1=ALU.add)
            link(ins)
            for t in range(TT):
                ins = dve.tensor_scalar(cum[:, t, :], cum[:, t, :], ngt[:, t:t + 1], float(TOP), ALU.add, ALU.is_le)
            link(ins)
            link(dve.tensor_tensor(eq[:, :, :], eq[:, :, :], cum[:, :, :], ALU.mult))
            dve.tensor_tensor(chosen[:, :, :], eq[:, :, :], gt[:, :, :], ALU.add).then_inc(s_cho, 1)
            dve.wait_ge(s_cho, 1)
            dve.wait_ge(s_le, 1)
            link(dve.tensor_tensor(ex[:, :, :], ex[:, :, :], chosen[:, :, :], ALU.mult))
            link(dve.tensor_reduce(ngt[:, :], ex[:, :, :], AX.X, ALU.add))
            link(dve.reciprocal(ngt[:, :], ngt[:, :]))
            link(dve.tensor_tensor(gates[:, :, :], ex[:, :, :],
                                   ngt[:, :].rearrange("p (t a) -> p t a", a=1).broadcast_to([P, TT, E]), ALU.mult))
            dve.wait_ge(s_cnt, 1)
            link(dve.tensor_copy(cnt[:, :], bank[5][0:E, 2 * E:2 * E + 1]))
            dve.tensor_scalar(more[:, :], block_c[:, :], cnt[:, 0:1], None, ALU.is_lt).then_inc(s_more, 1)
            dve.scalar_tensor_tensor(out=rank1[:, :, :], in0=bank[5][:, 0:TT * E].rearrange("p (t e) -> p t e", t=TT),
                                     scalar=1.0, in1=chosen[:, :, :], op0=ALU.add, op1=ALU.mult).then_inc(s_gtk, 1)
            dve.wait_ge(s_gt, 1)
            dve.tensor_copy(gates_t[:, :, :], bank[6][0:E, 0:T].rearrange("e (t p) -> e t p", t=TT)).then_inc(s_gtk, 1)
            dve.wait_ge(s_pref, 1)
            link(dve.tensor_copy(place[:, :], bank[7][0:E, 0:BLOCKS - 1]))
            tot = BLOCKS - 1
            for b in range(1, BLOCKS - 1):
                for a in range(b):
                    link(dve.tensor_tensor(place[:, b:b + 1], place[:, b:b + 1], bank[7][0:E, tot + a:tot + a + 1], ALU.add))
            link(dve.scalar_tensor_tensor(out=place[:, :], in0=place[:, :], scalar=1.0, in1=more[:, :],
                                          op0=ALU.add, op1=ALU.mult))
            for b in range(BLOCKS - 1):
                ins = dve.tensor_scalar(hot[:, b, :], extra1[:, :], place[:, b:b + 1], None, ALU.is_equal)
            ins.then_inc(s_hot, 1)
            dve.wait_ge(s_tab, 1)
            dve.wait_ge(s_const, 3)
            for a in range(2):
                link(dve.tensor_copy(table_f[0:1, a * TABLE + E:a * TABLE + E + EXTRA], bank[7][0:1, 16 + a * EXTRA:16 + (a + 1) * EXTRA]))
            link(dve.tensor_copy(n_f[0:1, :], bank[7][0:1, 64:64 + BLOCKS - 1]))
            link(dve.tensor_copy(table[0:1, :], table_f[0:1, :]))
            link(dve.tensor_reduce(cnt[0:1, :], n_f[0:1, :], AX.X, ALU.add))
            dve.tensor_scalar(n_items[0:1, :], cnt[0:1, :], float(E), None, ALU.add).then_inc(s_items, 1)

            for t in range(TT):
                dve.wait_ge(s_h2hi, t + 1)
                dve.tensor_tensor(h2_lo[:, t, :], h_row[:, t, :], h2_hi[:, t, :], ALU.subtract).then_inc(s_h2lo, 1)
            dve.wait_ge(s_h2lo, TT)
            dve.sem_inc(s_mixed, 1)

            def place_slots(e, boff):
                for t in range(TT):
                    dve.tensor_scalar(p_row[:, t, :], slot1[:, :, :].rearrange("p b s -> p (b s)")[:, ds(boff, P)],
                                      rank1[:, t, ds(e, 1)], None, ALU.is_equal)
                dve.tensor_copy(gate_c[:, :], gates[:, :, ds(e, 1)].rearrange("p t e -> p (t e)")).then_inc(s_p, 1)

            def pick_bias(e):
                return dve.tensor_copy(bias_e[:, :, :], bias_t[:, :, :, ds(e, 1)].rearrange("p a f e -> p a (f e)"))

            dve.wait_ge(s_items, 1)
            n = dve.value_load(n_items[0:1, 0:1], min_val=E, max_val=E + EXTRA)
            dve.wait_ge(s_btk, 1)
            place_slots(0, 0)
            link(pick_bias(0))
            dve.sem_inc(s_gur, 1)
            base = steps[0]
            PER = 14

            with dve.Fori(0, n) as it:
                k = [0]

                def step(ins):
                    k[0] += 1
                    ins.then_inc(s_dve, 1)
                    dve.wait_ge(s_dve, it * PER + (base + k[0]))

                def lo(u):
                    i = SPLIT.index(u)
                    dve.wait_ge(s_hi, it * len(SPLIT) + (i + 1))
                    dve.tensor_tensor(w_lo[:, i % BUFS, :], ring[:, item_slot(u // 4), (u % 4) * UNIT:(u % 4 + 1) * UNIT],
                                      w_hi[:, i % BUFS, :], ALU.subtract).then_inc(s_lo, 1)

                def swiglu_first(h):
                    dve.wait_ge(s_gu, it * 4 + (2 + 2 * h + 2))
                    step(dve.tensor_tensor(gu_b[:, :, :, :],
                                           bank[2][:, :].rearrange("p (a f s) -> p a f s", a=2, f=4),
                                           bias_e[:, :, 4 * h:4 * h + 4].rearrange("p a (f s) -> p a f s", s=1)
                                           .broadcast_to([P, 2, 4, SLOTS]), ALU.add))
                    dve.sem_inc(s_gur, 1)
                    dve.tensor_scalar(g_lim[:, :, :], gu_b[:, 0, :, :], LIMIT, None, ALU.min).then_inc(s_gl, 1)
                    dve.wait_ge(s_gl, it * 2 + (h + 1))
                    step(dve.tensor_scalar(u_lim[:, :, :], gu_b[:, 1, :, :], LIMIT, -LIMIT, ALU.min, ALU.max))
                    step(dve.scalar_tensor_tensor(out=u_lim[:, :, :], in0=u_lim[:, :, :], scalar=1.0,
                                                  in1=g_lim[:, :, :], op0=ALU.add, op1=ALU.mult))

                def swiglu_second(h):
                    dve.wait_ge(s_ge, it * 2 + (h + 1))
                    step(dve.tensor_scalar(act[:, :, :], g_exp[:, :, :], 1.0, None, ALU.add))
                    step(dve.reciprocal(act[:, :, :], act[:, :, :]))
                    step(dve.tensor_tensor(act[:, :, :], act[:, :, :], u_lim[:, :, :], ALU.mult))
                    step(dve.tensor_copy(a_sp[:, 4 * h:4 * h + 4, 0, :], act[:, :, :]))
                    dve.tensor_tensor(a_sp[:, 4 * h:4 * h + 4, 1, :], act[:, :, :], a_sp[:, 4 * h:4 * h + 4, 0, :],
                                      ALU.subtract).then_inc(s_a, 1)

                e_next = dve.value_load(table[0:1, ds(it + 1, 1)], min_val=0, max_val=E - 1)
                b_next = dve.value_load(table[0:1, ds(it + (TABLE + 1), 1)], min_val=0, max_val=(BLOCKS - 1) * P)
                for u in range(2, 10):
                    lo(u)
                dve.wait_ge(s_pt, it + 1)
                place_slots(e_next, b_next)
                for u in range(10, 13):
                    lo(u)
                swiglu_first(0)
                lo(13)
                swiglu_second(0)
                lo(14)
                lo(15)
                lo(18)
                swiglu_first(1)
                lo(19)
                swiglu_second(1)
                for u in range(20, 24):
                    lo(u)
                pick_bias(e_next)
                for i, nn in enumerate((1, 0)):
                    dve.wait_ge(s_zh, it * 2 + (i + 1))
                    dve.scalar_tensor_tensor(out=z_lo[:, nn * 512:(nn + 1) * 512], in0=bank[nn][:, :],
                                             scalar=gate_s[:, 0:1], in1=z_hi[:, nn * 512:(nn + 1) * 512],
                                             op0=ALU.mult, op1=ALU.subtract).then_inc(s_zl, 1)
                assert k[0] == PER, k[0]

            dve.wait_ge(s_y, n)
            for t in range(TT):
                for nn in range(2):
                    c = slice(nn * 512, (nn + 1) * 512)
                    dve.tensor_tensor(xs[:, t, c], xs[:, t, c], y_ps[t][nn][:, :], ALU.add).then_inc(s_x3, 1)
            dve.wait_ge(s_ss, 6)
            dve.tensor_scalar(var[:, :], ss[:, :], 1.0 / D, EPS, ALU.mult, ALU.add).then_inc(s_var, 1)
            dve.wait_ge(s_rs, 3)
            for op in range(4):
                dve.wait_ge(s_last, op) if op else None
                if op == 0:
                    ins = dve.tensor_tensor(tmp2[:, :], rstd[:, :], rstd[:, :], ALU.mult)
                elif op == 1:
                    ins = dve.tensor_tensor(tmp2[:, :], tmp2[:, :], var[:, :], ALU.mult)
                elif op == 2:
                    ins = dve.tensor_scalar(tmp2[:, :], tmp2[:, :], -0.5, 1.5, ALU.mult, ALU.add)
                else:
                    ins = dve.tensor_tensor(rstd[:, :], rstd[:, :], tmp2[:, :], ALU.mult)
                ins.then_inc(s_last, 1)
            dve.wait_ge(s_last, 4)
            dve.wait_ge(s_gfin, 16)
            for t in range(TT):
                dve.scalar_tensor_tensor(out=y_out[:, t, :], in0=xs[:, t, :], scalar=rstd[:, t:t + 1],
                                         in1=g_bc[:, :], op0=ALU.mult, op1=ALU.mult).then_inc(s_fin, 1)

        @block.tensor
        def _(pe):
            mm = nc.tensor.matmul

            pe.wait_ge(s_const, 1)
            pe.wait_ge(s_small, 16 * 7)
            nc.tensor.transpose(bank[4][:, 0:NCOLS], rows[:, :], ident[0:NCOLS, 0:NCOLS]).then_inc(s_small_t, 1)

            def transposes(ready, n0):
                pe.wait_ge(ready, TT)
                for i in range(4):
                    for k in range(2):
                        for t in range(TT):
                            ins = nc.tensor.transpose(bank[i][:, k * T + t * P:k * T + (t + 1) * P],
                                                      h_row[:, t, (2 * i + k) * P:(2 * i + k + 1) * P], ident[:, :])
                    ins.then_inc(s_tr, 1)

            transposes(s_h, 0)
            pe.wait_ge(s_trA, 2)
            pe.wait_ge(s_trD, 2)

            def project(n):
                what, i = PROJ[n]
                dst = bank[n % 4]
                if n >= 4:
                    pe.wait_ge(s_pk, n - 3)
                if what == "gk":
                    for k in range(KT):
                        ins = mm(dst[0:RANK, 0:T], wgk[:, k, :], h_t[:, k, :], start=k == 0, stop=k == KT - 1)
                    ins.then_inc(s_pj, 1)
                    return
                if i == 0:
                    pe.wait_ge(s_slot[slot_of(what)], 16)
                w = chunk_view(what, KT)
                if what == VV:
                    for k in range(KT):
                        ins = mm(dst[:, :], h_t[:, k, i * P:(i + 1) * P], w[:, k, :], start=k == 0, stop=k == KT - 1)
                else:
                    for m in range(2):
                        for k in range(KT):
                            ins = mm(dst[:, m * T:(m + 1) * T], w[:, k, (2 * i + m) * P:(2 * i + m + 1) * P],
                                     h_t[:, k, :], start=k == 0, stop=k == KT - 1)
                ins.then_inc(s_pj, 1)
                if i == 1:
                    pe.wait_ge(s_pj, n + 1)
                    pe.sem_inc(s_used, 1)

            for n in range(3):
                project(n)
            pe.wait_ge(s_pk, 3)
            pe.wait_ge(s_trD, 2)
            for a in range(PAIRS):
                ins = mm(bank[4][:, a * T:(a + 1) * T], wgu[:, a, :], gkl[:, :], start=True, stop=True)
            ins.then_inc(s_gk, 1)
            project(3)
            project(4)
            pe.wait_ge(s_dec, 4)
            for t in range(TT):
                for a in range(PAIRS):
                    ins = nc.tensor.transpose(bank[5][:, (t * PAIRS + a) * P:(t * PAIRS + a + 1) * P],
                                              k_rem[:, a, t * P:(t + 1) * P], ident[:, :])
            ins.then_inc(s_kt, 1)
            project(5)
            project(6)
            pe.wait_ge(s_krow, 1)
            pe.wait_ge(s_pk, 5)
            for n in range(NCH - 1):
                r = slice(CH * (n % 2), CH * (n % 2 + 1))
                for a in range(PAIRS):
                    ins = mm(bank[(6, 7, 4)[n]][:, a * 2 * DV:(a + 1) * 2 * DV], k_row[r, n // 2, a * P:(a + 1) * P],
                             v_row[r, n // 2, a * 2 * DV:(a + 1) * 2 * DV], start=True, stop=True)
                ins.then_inc(s_kv, 1)
            for t in range(TT):
                if t == 1:
                    pe.wait_ge(s_st, 1)
                for h in range(HEADS):
                    ins = mm(bank[5 + t][:, h * P:(h + 1) * P], k_dec[:, h // 2, h % 2, t * P:(t + 1) * P],
                             q_dec[:, h // 2, t * P:(t + 1) * P], start=True, stop=True)
                ins.then_inc(s_sc, 1)
            project(7)
            project(8)
            pe.wait_ge(s_mask, 2)
            pe.wait_ge(s_st, 3)
            for i in range(2):
                dst = bank[(7, 4)[i]]
                for h in range(2 * i, 2 * i + 2):
                    for t in range(TT):
                        c0 = (h % 2) * T + t * P
                        mm(dst[:, c0:c0 + P], v_row[:, t, h * DV:(h + 1) * DV], sc[:, t, h, :], start=True, stop=False)
                        for n in range(2 * t, 2 * t + 2):
                            if n == 0:
                                continue
                            c1 = c0 + CH * (n % 2)
                            ins = mm(dst[:, c1:c1 + CH], state[:, n - 1, h // 2, h % 2, :],
                                     q_dec[:, h // 2, n * CH:(n + 1) * CH], start=False, stop=n % 2 == 1)
                ins.then_inc(s_o, 1)
            project(9)
            project(10)
            for i in range(2):
                pe.wait_ge(s_osq, i + 1)
                pe.wait_ge(s_sck, 2 * (i + 1))
                mm(bank[5 + i][:, :], ones[:, :], o_sq[:, 2 * i:2 * i + 2, :].rearrange("p a t -> p (a t)"),
                   start=True, stop=True).then_inc(s_ms, 1)
            project(11)
            project(12)
            pe.wait_ge(s_ygla, 2)
            for n in range(2):
                pe.wait_ge(s_slot[slot_of(WO + n)], 32)
                w = chunk_view(WO + n, KT)
                for t in range(TT):
                    order = list(range(CT, KT)) + list(range(CT))
                    for j, k in enumerate(order):
                        if n == 0 and t == 0 and k in (0, 2):
                            pe.wait_ge(s_yconv, k // 2 + 1)
                        ins = mm(bank[OUT_BANK[2 * n + t]][:, :], y_t[:, k, t * P:(t + 1) * P], w[:, k, :],
                                 start=j == 0, stop=j == KT - 1)
                    ins.then_inc(s_op, 1)
                pe.wait_ge(s_op, 2 * n + 2)
                pe.sem_inc(s_used, 1)
            pe.wait_ge(s_bias, 32)
            for i in range(2 * F // P):
                ins = nc.tensor.transpose(bank[7][:, i * E:(i + 1) * E], bgu[:, i * P:(i + 1) * P], ident[0:E, 0:E])
            ins.then_inc(s_bt, 1)
            pe.wait_ge(s_late, 16 * 3)
            transposes(s_h2, 4)
            pe.wait_ge(s_trA, 4)
            pe.wait_ge(s_trD, 4)
            for t in range(TT):
                for k in range(KT):
                    ins = mm(bank[4][:, t * E:(t + 1) * E], h_t[:, k, t * P:(t + 1) * P], wr[:, k, :],
                             start=k == 0, stop=k == KT - 1)
            ins.then_inc(s_lg, 1)
            pe.wait_ge(s_cho, 1)
            pe.wait_ge(s_const, 3)
            mm(bank[5][:, 0:E], before[:, :], chosen[:, 0, :], start=True, stop=True)
            mm(bank[5][:, E:2 * E], before[:, :], chosen[:, 1, :], start=True, stop=False)
            mm(bank[5][:, E:2 * E], ones[:, :], chosen[:, 0, :], start=False, stop=True)
            for t in range(TT):
                ins = mm(bank[5][0:E, 2 * E:2 * E + 1], chosen[:, t, :], ones[:, 0:1], start=t == 0, stop=t == TT - 1)
            ins.then_inc(s_cnt, 1)
            pe.wait_ge(s_more, 1)
            pe.wait_ge(s_btk, 1)
            nb = BLOCKS - 1
            mm(bank[7][0:E, 0:nb], before[0:E, 0:E], more[:, :], start=True, stop=True)
            mm(bank[7][0:E, nb:2 * nb], ones[0:E, 0:E], more[:, :], start=True, stop=True)
            mm(bank[7][0:1, 64:64 + nb], ones[0:E, 0:1], more[:, :], start=True, stop=True).then_inc(s_pref, 1)
            pe.wait_ge(s_gtk, 1)
            for t in range(TT):
                ins = nc.tensor.transpose(bank[6][0:E, t * P:(t + 1) * P], gates[:, t, :], ident[:, :])
            ins.then_inc(s_gt, 1)
            pe.wait_ge(s_hot, 1)
            for a in range(2):
                for b in range(nb):
                    ins = mm(bank[7][0:1, 16 + a * EXTRA:16 + (a + 1) * EXTRA],
                             exp_c[:, 0:1] if a == 0 else boff_c[:, b:b + 1], hot[:, b, :],
                             start=b == 0, stop=b == nb - 1)
            ins.then_inc(s_tab, 1)

            pe.wait_ge(s_gtk, 2)
            pe.wait_ge(s_items, 1)
            for t in range(TT):
                for nn in range(2):
                    ins = mm(y_ps[t][nn][:, :], gates_t[:, t, :], bdn[:, nn * 512:(nn + 1) * 512], start=True, stop=True)
            ins.then_inc(s_mixed, 1)
            n = pe.value_load(n_items[0:1, 0:1], min_val=E, max_val=E + EXTRA)
            pe.wait_ge(s_h2lo, TT)
            pe.sem_inc(s_free, AHEAD)
            pe.sem_inc(s_gu, 2)

            def gather(it, half, dst):
                for k in range(4):
                    kk = 4 * half + k
                    for part, src in enumerate((h2_hi, h2_lo)):
                        for t in range(TT):
                            ins = mm(dst[:, (2 * k + part) * SLOTS:(2 * k + part + 1) * SLOTS],
                                     src[:, t, kk * P:(kk + 1) * P], p_row[:, t, 0:SLOTS], start=t == 0, stop=t == TT - 1)
                ins.then_inc(s_xg, 1)

            pe.wait_ge(s_p, 1)
            gather(0, 0, bank[3])
            gather(0, 1, bank[0])

            with pe.Fori(0, n) as it:
                def unit(u, last=False):
                    j, uu = u // 4, u % 4
                    slot = ring[:, item_slot(j), uu * UNIT:(uu + 1) * UNIT]
                    if u in WHOLE:
                        if uu == 0:
                            pe.wait_ge(s_slot[item_slot(j)], item_loaded(it, j))
                        parts = [slot]
                    else:
                        i = SPLIT.index(u)
                        pe.wait_ge(s_lo, it * len(SPLIT) + (i + 1))
                        parts = [w_hi[:, i % BUFS, :], w_lo[:, i % BUFS, :]]
                    whole = u in WHOLE

                    def stationary(ap):
                        return ap.bitcast(f32) if whole else ap

                    if j < 4:
                        for kk in range(2):
                            k = 2 * uu + kk
                            lhs = stationary(x_sp[:, k, :, :].rearrange("p a s -> p (a s)"))
                            for q, w in enumerate(parts):
                                ins = mm(bank[j % 2][:, :], lhs, w[:, kk * 512:(kk + 1) * 512],
                                         start=k == 0 and q == 0, stop=k == KT - 1 and q == len(parts) - 1)
                    else:
                        k = 4 * (j - 4) + uu
                        lhs = stationary(a_sp[:, k, :, :].rearrange("p a s -> p (a s)"))
                        for nn in (1, 0):
                            for q, w in enumerate(parts):
                                ins = mm(bank[nn][:, :], lhs, w[:, nn * 512:(nn + 1) * 512],
                                         start=k == 0 and q == 0, stop=k == KT - 1 and q == len(parts) - 1)
                            if k == KT - 1 and nn == 1:
                                ins.then_inc(s_dn, 1)
                    if last:
                        ins.then_inc(s_used, 1)
                    elif not whole:
                        ins.then_inc(s_free, 1)

                def chunk(j):
                    for uu in range(4):
                        unit(4 * j + uu, last=uu == 3)

                def fold_up(c):
                    pe.wait_ge(s_up, it * 4 + (c + 1))
                    if c % 2 == 0:
                        pe.wait_ge(s_gur, it * 2 + (c // 2 + 1))
                    for f in range(4):
                        o = (c % 2) * 4 * SLOTS + f * SLOTS
                        ins = mm(bank[2][:, o:o + SLOTS], up_sb[:, c % 2, f * P:(f + 1) * P], fold[:, :],
                                 start=True, stop=True)
                    ins.then_inc(s_gu, 1)

                pe.wait_ge(s_xs, it * 2 + 2)
                chunk(0)
                for t in range(TT):
                    nc.tensor.transpose(bank[3][:, t * P:(t + 1) * P], p_row[:, t, :].bitcast(f32), ident[:, :])
                for t in range(TT):
                    ins = mm(bank[3][:, T:T + 1], p_row[:, t, :].bitcast(f32), gate_c[:, t:t + 1],
                             start=t == 0, stop=t == TT - 1)
                ins.then_inc(s_pt, 1)
                chunk(1)
                fold_up(0)
                chunk(2)
                fold_up(1)
                chunk(3)
                fold_up(2)
                pe.wait_ge(s_p, it + 2)
                pe.wait_ge(s_ptk, it + 1)
                gather(it + 1, 0, bank[3])
                fold_up(3)
                gather(it + 1, 1, bank[0])
                pe.wait_ge(s_a, it * 2 + 1)
                pe.wait_ge(s_xs, it * 2 + 4)
                chunk(4)
                pe.wait_ge(s_a, it * 2 + 2)
                chunk(5)
                for i, nn in enumerate((1, 0)):
                    pe.wait_ge(s_zl, it * 2 + (i + 1))
                    for t in range(TT):
                        for q, z in enumerate((z_hi, z_lo)):
                            ins = mm(y_ps[t][nn][:, :], p_t[:, t * P:(t + 1) * P], z[:, nn * 512:(nn + 1) * 512],
                                     start=False, stop=False, skip_group_check=True)
                ins.then_inc(s_y, 1)


_INS = ["x", "norm_mix_g", "w_in", "conv_w", "w_gk_up", "b_gk_up", "gla_norm_g", "w_out", "norm_ffn_g",
        "w_router", "b_router", "w_gate_up", "b_gate_up", "w_down", "b_down", "norm_final_g"]


def kernel(**inputs):
    import numpy as _np
    import concourse.bacc as _bacc
    from concourse import mybir as _mybir
    from concourse.bass_utils import run_bass_kernel_spmd as _run

    nc = _bacc.Bacc("TRN2", target_bir_lowering=False, num_devices=1)
    arrays, args = {}, []
    for name in _INS:
        a = _np.ascontiguousarray(inputs[name])
        arrays[f"in_{name}"] = a
        args.append(nc.dram_tensor(f"in_{name}", a.shape, _mybir.dt.from_np(a.dtype), kind="ExternalInput").ap())
    args.append(nc.dram_tensor("out", (1, T, D), _mybir.dt.float32, kind="ExternalOutput").ap())
    build(nc, *args)
    r = _run(nc, [arrays], core_ids=[0])
    return r.results[0]["out"]
```

```python
import numpy as np
import concourse.bass as bass
from concourse import mybir
from contextlib import ExitStack

P = 128
D = 1024
T = 256
TT = T // P
KT = D // P
CONV = 512
CT = CONV // P
TAPS = 3
HEADS = 4
DK = 64
DV = 128
PAIRS = HEADS // 2
CH = 64
NCH = T // CH
RANK = 16
NORMALIZER = 16.0
E = 32
TOP = 4
F = 1024
LIMIT = 7.0
ALPHA = 1.702
EPS = 1e-5
SLOTS = 64
BLOCKS = T // SLOTS
EXTRA = T * TOP // SLOTS
TABLE = E + 2 * EXTRA
NCOLS = 2 + 1 + TAPS * CT + KT
FFN0 = 2 + 1 + TAPS * CT

CHUNK = 4096
RING = 6
MIX_CHUNKS = 8
QK, VV, GG, UU, CC, BB, WO = range(7)
ITEM_CHUNKS = 6
UNIT = 1024
UNITS = ITEM_CHUNKS * CHUNK // UNIT
WHOLE = (0, 1, 18, 19)
SPLIT = [u for u in range(UNITS) if u not in WHOLE]
BUFS = 4
assert len(SPLIT) % BUFS == 0
FREED = [u for u in SPLIT if u % 4 != 3]
AHEAD = sum(u % 4 != 3 for u in SPLIT[-BUFS:])


def slot_of(chunk):
    return chunk % RING


def build(nc, x, norm_mix_g, w_in, conv_w, w_gk_up, b_gk_up, gla_norm_g, w_out, norm_ffn_g,
          w_router, b_router, w_gate_up, b_gate_up, w_down, b_down, norm_final_g, out):
    f32 = mybir.dt.float32
    f32r = mybir.dt.float32r
    i32 = mybir.dt.int32
    ALU = mybir.AluOpType
    ACT = mybir.ActivationFunctionType
    AX = mybir.AxisListType
    ds = bass.ds

    x_v = x[0].rearrange("(t p) d -> p t d", p=P)
    out_v = out[0].rearrange("(t p) d -> p t d", p=P)
    win_v = w_in[0].rearrange("(k p) n -> p k n", p=P)
    wout_v = w_out[0].rearrange("(k p) n -> p k n", p=P)
    wr_v = w_router[0].rearrange("(k p) n -> p k n", p=P)
    gu_v = w_gate_up[0].rearrange("e (k p) n -> p e k n", p=P)
    dn_v = w_down[0].rearrange("e (k p) n -> p e k n", p=P)
    col0 = {UU: 0, BB: CONV, CC: 2 * CONV, QK: 3 * CONV, VV: 4 * CONV, GG: 5 * CONV}
    GKLOW0 = 6 * CONV

    ctx = ExitStack()
    with ctx:
        def sb(name, shape, dt=f32, scope=ctx):
            return scope.enter_context(nc.sbuf_tensor(name, shape, dt))

        def sem(name):
            return ctx.enter_context(nc.semaphore(name))

        ring = sb("ring", [P, RING, CHUNK])
        xs = sb("x_sb", [P, TT, D])
        g_bc = sb("g_bc", [P, D])
        ident = sb("ident", [P, P])
        ones = sb("ones", [P, P])
        before = sb("before", [P, P])
        fold = sb("fold", [P, SLOTS])
        slot1 = sb("slot1", [P, BLOCKS, P])
        eps_c = sb("eps_c", [P, 1])
        one_c = sb("one_c", [P, 1])
        ss = sb("ss", [P, TT])
        var = sb("var", [P, TT])
        lnv = sb("lnv", [P, TT])
        rstd = sb("rstd", [P, TT])
        tmp2 = sb("tmp2", [P, TT])
        gates = sb("gates", [P, TT, E])
        rank1 = sb("rank1", [P, TT, E])
        bias_t = sb("bias_t", [P, 2, F // P, E])
        bias_e = sb("bias_e", [P, 2, F // P])
        table = sb("table", [1, 2 * TABLE], i32)
        n_items = sb("n_items", [1, 1], i32)

        router = ExitStack()
        mixer = ExitStack()
        late = ExitStack()

        def rb(name, shape, dt=f32):
            return sb(name, shape, dt, router)

        h_t = rb("h_t", [P, KT, T])
        h_row = rb("h_row", [P, TT, D])
        y_t = h_row[:, :, :].rearrange("p t (k n) -> p (t k) n", n=T)
        gffn_bc = rb("gffn_bc", [P, D])
        wr = rb("wr", [P, KT, E])
        wr_g = rb("wr_g", [P, KT, E])
        br_bc = rb("br_bc", [P, E])
        lg = rb("lg", [P, TT, E])
        lmax = rb("lmax", [P, TT, 8])
        ngt = rb("ngt", [P, TT])
        gt = rb("gt", [P, TT, E])
        eq = rb("eq", [P, TT, E])
        cum = rb("cum", [P, TT, E])
        chosen = rb("chosen", [P, TT, E])
        ex = rb("ex", [P, TT, E])
        gates_t = rb("gates_t", [E, TT, P])
        cnt = rb("cnt", [E, 1])
        more = rb("more", [E, BLOCKS - 1])
        block_c = rb("block_c", [E, BLOCKS - 1])
        boff_c = rb("boff_c", [E, BLOCKS - 1])
        exp_c = rb("exp_c", [E, 1])
        place = rb("place", [E, BLOCKS - 1])
        extra1 = rb("extra1", [E, EXTRA])
        hot = rb("hot", [E, BLOCKS - 1, EXTRA])
        table_f = rb("table_f", [1, 2 * TABLE])
        n_f = rb("n_f", [1, BLOCKS - 1])

        def mb(name, shape, dt=f32):
            return sb(name, shape, dt, mixer)

        wgk = mb("wgk", [P, KT, RANK])
        wgu = mb("wgu", [RANK, PAIRS, P])
        rows = mb("rows", [NCOLS, P])
        cols = mb("cols", [P, NCOLS])
        gkl = mb("gkl", [RANK, T])
        gk = mb("gk", [P, PAIRS, T])
        la = mb("la", [P, PAIRS, T])
        lb = mb("lb", [P, PAIRS, T])
        e_pos = mb("e_pos", [P, PAIRS, T])
        e_neg = mb("e_neg", [P, PAIRS, T])
        e_rem = mb("e_rem", [P, PAIRS, T])
        qk = mb("qk", [P, 2, PAIRS, T])
        o_r = qk[:, :, :, :].rearrange("p a b t -> p (a b) t")
        q_dec = mb("q_dec", [P, PAIRS, T])
        k_dec = mb("k_dec", [P, PAIRS, 2, T])
        o_sq = k_dec[:, :, :, :].rearrange("p a b t -> p (a b) t")
        k_rem = mb("k_rem", [P, PAIRS, T])
        k_row = mb("k_row", [P, TT, PAIRS * P])
        v_row = mb("v_row", [P, TT, HEADS * DV])
        g_t = mb("g_t", [P, HEADS, T])
        sil = mb("sil", [P, HEADS, T])
        state = mb("state", [P, NCH - 1, PAIRS, 2, DV])
        sc = mb("sc", [P, TT, HEADS, P])
        reset = mb("reset", [P, PAIRS * NCH, CH])
        u_t = mb("u_t", [P, CT, T])
        u_pad = mb("u_pad", [P, CT, T + TAPS - 1])
        conv = mb("conv", [P, CT, T])
        mixer.close()

        bgu = sb("bgu", [E, 2 * F], f32, late)
        bdn = sb("bdn", [E, D], f32, late)
        late.close()
        router.close()

        w_hi = sb("w_hi", [P, BUFS, UNIT], f32r)
        w_lo = sb("w_lo", [P, BUFS, UNIT], f32r)
        z_hi = sb("z_hi", [P, D], f32r)
        z_lo = sb("z_lo", [P, D], f32r)
        h2 = sb("h2", [P, TT, D])
        x_sp = sb("x_sp", [P, KT, 2, SLOTS], f32r)
        p_row = sb("p_row", [P, TT, P], f32r)
        gate_c = sb("gate_c", [P, TT])
        up_sb = sb("up_sb", [P, 2, 512])
        gu_b = sb("gu_b", [P, 2, 4, SLOTS])
        g_lim = sb("g_lim", [P, 4, SLOTS])
        u_lim = sb("u_lim", [P, 4, SLOTS])
        g_sig = sb("g_sig", [P, 4, SLOTS])
        act = sb("act", [P, 4, SLOTS])
        a_sp = sb("a_sp", [P, F // P, 2, SLOTS], f32r)
        p_t = sb("p_t", [P, T], f32r)
        gate_s = sb("gate_s", [P, 1])
        y_out = sb("y_out", [P, TT, D])

        bank = [ctx.enter_context(nc.psum_tensor(f"bank{i}", [P, 512], f32)) for i in range(8)]
        y_ps = [[bank[4 + 2 * t + n] for n in range(2)] for t in range(TT)]

        s_x = [sem(f"x{t}_loaded") for t in range(TT)]
        s_gmix = sem("g_mix_loaded")
        s_small = sem("small_loaded")
        s_late = sem("router_weights_loaded")
        s_bias = sem("expert_biases_loaded")
        s_gfin = sem("g_final_loaded")
        s_slot = [sem(f"slot{i}_loaded") for i in range(RING)]
        s_used = sem("chunk_used")
        s_const = sem("consts_ready")
        s_ss = sem("squares_summed")
        s_var = sem("variance_ready")
        s_rs = sem("rsqrt_ready")
        s_lv = sem("log_variance_ready")
        s_sp = sem("softplus_step")
        s_ol = sem("o_log_ready")
        s_rr = sem("rsqrt_refined")
        s_wr = sem("router_weights_scaled")
        s_h = sem("h_ready")
        s_tr = sem("transposed")
        s_trA = sem("transposed_kept_act")
        s_trD = sem("transposed_kept_dve")
        s_small_t = sem("small_transposed")
        s_cols = sem("cols_ready")
        s_pj = sem("projected")
        s_pk = sem("projection_kept")
        s_gk = sem("gk_ready")
        s_gkb = sem("gk_biased")
        s_ln = sem("softplus_ready")
        s_cs = sem("log_sums_ready")
        s_ex = sem("decays_ready")
        s_dec = sem("decayed_ready")
        s_kt = sem("k_transposed")
        s_krow = sem("k_row_ready")
        s_kv = sem("kv_ready")
        s_st = sem("state_ready")
        s_sc = sem("scores_ready")
        s_sck = sem("scores_kept")
        s_mask = sem("scores_masked")
        s_o = sem("o_ready")
        s_osq = sem("o_squared")
        s_ms = sem("o_mean_ready")
        s_or = sem("o_rsqrt_ready")
        s_sg = sem("silu_exp_ready")
        s_ygla = sem("y_gla_ready")
        s_yconv = sem("y_conv_ready")
        s_op = sem("out_projected")
        s_x2 = sem("x2_ready")
        s_h2 = sem("h2_ready")
        s_bt = sem("bias_transposed")
        s_btk = sem("bias_t_ready")
        s_lg = sem("logits_ready")
        s_lgk = sem("logits_less_max")
        s_le = sem("logits_exp")
        s_cho = sem("chosen_ready")
        s_cnt = sem("counted")
        s_more = sem("more_ready")
        s_pref = sem("prefix_ready")
        s_hot = sem("hot_ready")
        s_tab = sem("table_summed")
        s_items = sem("items_ready")
        s_table = sem("table_ready")
        s_be = sem("bias_picked")
        s_gt = sem("gates_transposed")
        s_gtk = sem("gates_t_ready")
        s_mixed = sem("mixer_space_free")
        s_free = sem("split_buffer_free")
        s_hi = sem("w_hi_ready")
        s_lo = sem("w_lo_ready")
        s_p = sem("p_row_ready")
        s_xg = sem("x_gathered")
        s_xh = sem("x_high_ready")
        s_xs = sem("x_split")
        s_pt = sem("p_transposed")
        s_ptk = sem("p_t_ready")
        s_up = sem("up_kept")
        s_gu = sem("gate_up_folded")
        s_gur = sem("gate_up_biased")
        s_gl = sem("gate_limited")
        s_ul = sem("up_limited")
        s_um = sem("up_times_gate")
        s_sig = sem("sigmoid_ready")
        s_av = sem("activation_ready")
        s_ah = sem("activation_high_ready")
        s_a = sem("activation_split")
        s_dn = sem("down_first_ready")
        s_zh = sem("z_hi_ready")
        s_zl = sem("z_lo_ready")
        s_y = sem("item_added")
        s_x3 = sem("x3_ready")
        s_fin = sem("out_ready")
        s_out = sem("out_stored")
        s_dve = sem("dve_step")
        s_pool = sem("pool_step")

        PROJ = [(QK, 0), (QK, 1), ("gk", 0), (VV, 0), (VV, 1), (GG, 0), (GG, 1),
                (UU, 0), (UU, 1), (CC, 0), (CC, 1), (BB, 0), (BB, 1)]
        OUT_BANK = (5, 6, 1, 2)

        def two_tiles(n):
            return bank[n % 4][:, :].rearrange("p (a t) -> p a t", a=2)

        def chunk_view(c, k):
            return ring[:, slot_of(c), :].rearrange("p (k n) -> p k n", k=k)

        def item_slot(j):
            return slot_of(MIX_CHUNKS + j)

        def item_loaded(it, j):
            return (it + (MIX_CHUNKS + j) // RING + 1) * 16

        block = ctx.enter_context(nc.Block())

        @block.sync
        def _(sp):
            for t in range(TT):
                sp.dma_start(xs[:, t, :], x_v[:, t, :]).then_inc(s_x[t], 16)
            sp.wait_ge(s_small, 16 * 8)
            sp.wait_ge(s_gmix, 16)
            for c in range(MIX_CHUNKS):
                if c >= RING:
                    sp.wait_ge(s_used, c - RING + 1)
                if c < WO:
                    src = win_v[:, :, col0[c]:col0[c] + 512]
                else:
                    src = wout_v[:, :, (c - WO) * 512:(c - WO + 1) * 512]
                sp.dma_start(chunk_view(c, KT), src).then_inc(s_slot[slot_of(c)], 16)

            def load_item(it, e):
                for j in range(ITEM_CHUNKS):
                    sp.wait_ge(s_used, it * ITEM_CHUNKS + (MIX_CHUNKS + j - RING + 1))
                    if j < 4:
                        c0 = (j % 2) * F + (j // 2) * 512
                        src = gu_v[:, ds(e, 1), :, c0:c0 + 512].rearrange("p e k n -> p (e k) n")
                        dst = ring[:, item_slot(j), :].rearrange("p (k n) -> p k n", k=KT)
                    else:
                        src = dn_v[:, ds(e, 1), 4 * (j - 4):4 * (j - 3), :].rearrange("p e k n -> p (e k) n")
                        dst = ring[:, item_slot(j), :].rearrange("p (k n) -> p k n", k=4)
                    sp.dma_start(dst, src).then_inc(s_slot[item_slot(j)], 16)

            with sp.Fori(0, E) as it:
                load_item(it, it)
            sp.wait_ge(s_items, 1)
            n = sp.value_load(n_items[0:1, 0:1], min_val=E, max_val=E + EXTRA)
            with sp.If(n > E):
                with sp.Fori(E, n) as it:
                    sp.wait_ge(s_table, 1)
                    e = sp.value_load(table[0:1, ds(it, 1)], min_val=0, max_val=E - 1)
                    load_item(it, e)
            for t in range(TT):
                sp.wait_ge(s_fin, t + 1)
                sp.dma_start(out_v[:, t, :], y_out[:, t, :]).then_inc(s_out, 16)
            sp.wait_ge(s_out, 16 * TT)

        @block.gpsimd
        def _(pool):
            steps = [0]

            def link(ins):
                steps[0] += 1
                ins.then_inc(s_pool, 1)
                pool.wait_ge(s_pool, steps[0])

            link(pool.memset(ident[:, :], 0.0))
            link(pool.affine_select(out=ident[:, :], in_=ident[:, :], compare_op=ALU.not_equal, fill=1.0,
                                    base=0, pattern=[[-1, P]], channel_multiplier=1))
            link(pool.memset(ones[:, :], 1.0))
            link(pool.memset(eps_c[:, :], EPS))
            pool.memset(one_c[:, :], 1.0).then_inc(s_const, 1)
            link(pool.memset(k_dec[:, :, :, :], 0.0))
            link(pool.memset(u_pad[:, :, 0:TAPS - 1], 0.0))
            link(pool.memset(state[:, :, :, :, :], 0.0))
            link(pool.memset(sc[:, :, :, :], 0.0))
            link(pool.memset(reset[:, :, :], 1.0))
            pool.affine_select(out=reset[:, :, :], in_=reset[:, :, :], compare_op=ALU.is_gt, fill=0.0,
                               base=0, pattern=[[0, PAIRS * NCH], [1, CH]], channel_multiplier=0).then_inc(s_const, 1)
            link(pool.affine_select(out=before[:, :], in_=ones[:, :], compare_op=ALU.is_gt, fill=0.0,
                                    base=0, pattern=[[1, P]], channel_multiplier=-1))
            link(pool.memset(fold[:, :], 0.0))
            for off in (0, SLOTS):
                link(pool.affine_select(out=fold[:, :], in_=fold[:, :], compare_op=ALU.not_equal, fill=1.0,
                                        base=-off, pattern=[[-1, SLOTS]], channel_multiplier=1))
            link(pool.iota(slot1[:, :, :], pattern=[[SLOTS, BLOCKS], [0, 2], [1, SLOTS]], base=1,
                           channel_multiplier=0, allow_small_or_imprecise_dtypes=True))
            link(pool.iota(block_c[:, :], pattern=[[SLOTS, BLOCKS - 1]], base=SLOTS,
                           channel_multiplier=0, allow_small_or_imprecise_dtypes=True))
            link(pool.iota(boff_c[:, :], pattern=[[P, BLOCKS - 1]], base=P,
                           channel_multiplier=0, allow_small_or_imprecise_dtypes=True))
            link(pool.iota(exp_c[:, :], pattern=[[0, 1]], base=0,
                           channel_multiplier=1, allow_small_or_imprecise_dtypes=True))
            link(pool.iota(extra1[:, :], pattern=[[1, EXTRA]], base=1,
                           channel_multiplier=0, allow_small_or_imprecise_dtypes=True))
            link(pool.memset(table_f[:, :], 0.0))
            pool.iota(table_f[:, 0:E], pattern=[[1, E]], base=0,
                      channel_multiplier=0, allow_small_or_imprecise_dtypes=True).then_inc(s_const, 1)
            for t in range(TT):
                pool.wait_ge(s_sck, 2 * (t + 1))
                pool.affine_select(out=sc[:, t, :, :], in_=sc[:, t, :, :], compare_op=ALU.is_ge, fill=0.0,
                                   base=0, pattern=[[0, HEADS], [1, P]], channel_multiplier=-1).then_inc(s_mask, 1)

        @block.scalar
        def _(act_e):
            act_e.preload_act_table_set("natural_log_exp_and_others")
            act_e.dma_start(wgk[:, :, :], win_v[:, :, GKLOW0:GKLOW0 + RANK]).then_inc(s_small, 16)
            act_e.dma_start(g_bc[:, :], norm_mix_g.partition_broadcast(P)[:, 0, :]).then_inc(s_gmix, 16)
            act_e.dma_start(rows[0:2, :], b_gk_up[0].rearrange("(a p) -> a p", p=P)).then_inc(s_small, 16)
            act_e.dma_start(rows[2:3, :], gla_norm_g).then_inc(s_small, 16)
            for i in range(TAPS):
                act_e.dma_start(rows[3 + i * CT:3 + (i + 1) * CT, :],
                                conv_w[0, i].rearrange("(a p) -> a p", p=P)).then_inc(s_small, 16)
            act_e.dma_start(rows[FFN0:NCOLS, :], norm_ffn_g[0].rearrange("(a p) -> a p", p=P)).then_inc(s_small, 16)
            act_e.dma_start(wgu[:, :, :], w_gk_up[0].rearrange("r (a p) -> r a p", p=P)).then_inc(s_small, 16)
            act_e.dma_start(gffn_bc[:, :], norm_ffn_g.partition_broadcast(P)[:, 0, :]).then_inc(s_late, 16)
            act_e.dma_start(wr[:, :, :], wr_v).then_inc(s_late, 16)
            act_e.dma_start(br_bc[:, :], b_router.partition_broadcast(P)[:, 0, :]).then_inc(s_late, 16)

            act_e.wait_ge(s_const, 1)

            def square_sum(t, junk):
                act_e.activation(junk, xs[:, t, :], ACT.Square, accum_out=ss[:, t:t + 1]).then_inc(s_ss, 1)

            def rsqrt(norm, t):
                n = norm * TT + t
                act_e.wait_ge(s_var, n + 1)
                act_e.activation(lnv[:, t:t + 1], var[:, t:t + 1], ACT.Ln).then_inc(s_lv, 1)
                act_e.wait_ge(s_lv, n + 1)
                act_e.activation(rstd[:, t:t + 1], lnv[:, t:t + 1], ACT.Exp, scale=-0.5).then_inc(s_rs, 1)

            for t in range(TT):
                act_e.wait_ge(s_x[t], 16)
                square_sum(t, h_row[:, t, :])
            for t in range(TT):
                rsqrt(0, t)
            for i in (0, 2):
                act_e.wait_ge(s_tr, i + 1)
                act_e.copy(h_t[:, 2 * i:2 * i + 2, :], bank[i][:, :].rearrange("p (a t) -> p a t", a=2)).then_inc(s_trA, 1)

            def keep(n):
                what, i = PROJ[n]
                src = bank[n % 4]
                two = src[:, :].rearrange("p (a t) -> p a t", a=2)
                act_e.wait_ge(s_pj, n + 1)
                if what == "gk":
                    o, src_ap = gkl[:, :], src[0:RANK, 0:T]
                elif what == VV:
                    o, src_ap = v_row[:, i, :], src[:, :]
                elif what == QK:
                    o, src_ap = qk[:, i, :, :], two
                else:
                    o, src_ap = {GG: g_t, UU: u_t}[what][:, 2 * i:2 * i + 2, :], two
                act_e.copy(o, src_ap).then_inc(s_pk, 1)

            for n in range(3):
                keep(n)
            act_e.wait_ge(s_gkb, 1)
            act_e.activation(la[:, :, :], gk[:, :, :], ACT.Abs).then_inc(s_sp, 1)
            act_e.wait_ge(s_sp, 1)
            act_e.activation(lb[:, :, :], la[:, :, :], ACT.Exp, scale=-1.0).then_inc(s_sp, 1)
            act_e.wait_ge(s_sp, 2)
            act_e.activation(la[:, :, :], lb[:, :, :], ACT.Ln, bias=one_c[:, 0:1]).then_inc(s_ln, 1)
            keep(3)
            act_e.wait_ge(s_cs, 1)
            act_e.activation(e_pos[:, :, :], lb[:, :, :], ACT.Exp, scale=1.0 / NORMALIZER).then_inc(s_ex, 1)
            act_e.activation(e_neg[:, :, :], lb[:, :, :], ACT.Exp, scale=-1.0 / NORMALIZER).then_inc(s_ex, 1)
            act_e.activation(e_rem[:, :, :], gk[:, :, :], ACT.Exp, scale=1.0 / NORMALIZER).then_inc(s_ex, 1)
            for n in range(4, 7):
                keep(n)
            act_e.wait_ge(s_pk, 7)
            act_e.activation(sil[:, :, :], g_t[:, :, :], ACT.Exp, scale=-1.0).then_inc(s_sg, 1)
            for n in range(7, 9):
                keep(n)
            for i in range(2):
                act_e.wait_ge(s_o, i + 1)
                act_e.activation(o_sq[:, 2 * i:2 * i + 2, :], bank[(7, 4)[i]][:, :].rearrange("p (a t) -> p a t", a=2),
                                 ACT.Square).then_inc(s_osq, 1)
            for i in range(2):
                act_e.wait_ge(s_ms, i + 1)
                o = o_r[:, 2 * i:2 * i + 2, :]
                act_e.activation(o, bank[5 + i][:, :].rearrange("p (a t) -> p a t", a=2), ACT.Ln,
                                 scale=1.0 / DV, bias=eps_c[:, 0:1]).then_inc(s_ol, 1)
                act_e.wait_ge(s_ol, i + 1)
                act_e.activation(o, o, ACT.Exp, scale=-0.5).then_inc(s_or, 1)
            act_e.wait_ge(s_yconv, 2)
            act_e.wait_ge(s_wr, 1)
            act_e.dma_start(bgu[:, :], b_gate_up[0]).then_inc(s_bias, 16)
            act_e.dma_start(bdn[:, :], b_down[0]).then_inc(s_bias, 16)
            for t in range(TT):
                act_e.wait_ge(s_x2, 2 * (t + 1))
                if t == 0:
                    act_e.wait_ge(s_op, 4)
                square_sum(t, h_row[:, t, :])
                rsqrt(1, t)
                for i in (0, 1):
                    act_e.wait_ge(s_tr, 4 + 2 * t + i + 1)
                    act_e.copy(h_t[:, 4 * i:4 * i + 4, t * P:(t + 1) * P],
                               bank[(0, 3)[i]][:, :].rearrange("p (a t) -> p a t", a=4)).then_inc(s_trA, 1)
            act_e.dma_start(g_bc[:, :], norm_final_g.rearrange("(a d) -> a d", a=1).partition_broadcast(P)[:, 0, :]).then_inc(s_gfin, 16)
            act_e.wait_ge(s_lgk, 1)
            act_e.activation(ex[:, :, :], ex[:, :, :], ACT.Exp).then_inc(s_le, 1)

            act_e.wait_ge(s_items, 1)
            n = act_e.value_load(n_items[0:1, 0:1], min_val=E, max_val=E + EXTRA)

            def keep_gathered(it):
                act_e.wait_ge(s_xg, it + 1)
                act_e.copy(x_sp[:, :, 0, :], bank[3][:, :].rearrange("p (k s) -> p k s", k=KT)).then_inc(s_xh, 1)

            keep_gathered(0)
            act_e.wait_ge(s_bt, 1)
            act_e.copy(bias_t[:, :, :, :].rearrange("p a f e -> p (a f e)"), bank[2][:, :]).then_inc(s_btk, 1)

            act_e.wait_ge(s_mixed, 2)
            act_e.preload_act_table_set("sigmoid_and_others")

            with act_e.Fori(0, n) as it:
                def hi(u):
                    i = SPLIT.index(u)
                    j = u // 4
                    act_e.wait_ge(s_slot[item_slot(j)], item_loaded(it, j))
                    v = SPLIT[i - BUFS]
                    back = 0 if i >= BUFS else 1
                    if v % 4 == 3:
                        act_e.wait_ge(s_used, it * ITEM_CHUNKS + (MIX_CHUNKS + v // 4 + 1 - back * ITEM_CHUNKS))
                    else:
                        act_e.wait_ge(s_free, it * len(FREED) + (AHEAD + FREED.index(v) + 1 - back * len(FREED)))
                    act_e.copy(w_hi[:, i % BUFS, :], ring[:, item_slot(j), (u % 4) * UNIT:(u % 4 + 1) * UNIT]).then_inc(s_hi, 1)

                def keep_up(c):
                    act_e.wait_ge(s_used, it * ITEM_CHUNKS + (MIX_CHUNKS + c + 1))
                    act_e.wait_ge(s_gu, it * 4 + (c + 1))
                    act_e.copy(up_sb[:, c % 2, :], bank[c % 2][:, :]).then_inc(s_up, 1)

                def sigmoid(h):
                    act_e.wait_ge(s_gl, it * 2 + (h + 1))
                    act_e.activation(g_sig[:, :, :], g_lim[:, :, :], ACT.Sigmoid, scale=ALPHA).then_inc(s_sig, 1)

                def act_high(h):
                    act_e.wait_ge(s_av, it * 2 + (h + 1))
                    act_e.copy(a_sp[:, 4 * h:4 * h + 4, 0, :], act[:, :, :]).then_inc(s_ah, 1)

                for u in range(2, 7):
                    hi(u)
                keep_up(0)
                hi(7)
                act_e.wait_ge(s_pt, it + 1)
                act_e.copy(p_t[:, :], bank[3][:, 0:T])
                act_e.copy(gate_s[:, :], bank[3][:, T:T + 1]).then_inc(s_ptk, 1)
                for u in range(8, 11):
                    hi(u)
                keep_up(1)
                for u in range(11, 15):
                    hi(u)
                sigmoid(0)
                keep_up(2)
                hi(15)
                act_high(0)
                hi(16)
                hi(17)
                hi(20)
                keep_up(3)
                hi(21)
                sigmoid(1)
                act_high(1)
                hi(22)
                hi(23)
                for i, nn in enumerate((1, 0)):
                    if i == 0:
                        act_e.wait_ge(s_dn, it + 1)
                        act_e.wait_ge(s_ptk, it + 1)
                    else:
                        act_e.wait_ge(s_used, it * ITEM_CHUNKS + (MIX_CHUNKS + ITEM_CHUNKS))
                    act_e.activation(z_hi[:, nn * 512:(nn + 1) * 512], bank[nn][:, :], ACT.Copy,
                                     scale=gate_s[:, 0:1]).then_inc(s_zh, 1)
                keep_gathered(it + 1)

            act_e.preload_act_table_set("natural_log_exp_and_others")
            for t in range(TT):
                act_e.wait_ge(s_x3, 2 * (t + 1))
                square_sum(t, y_out[:, t, :])
                rsqrt(2, t)

        @block.vector
        def _(dve):
            steps = [0]

            def link(ins):
                steps[0] += 1
                ins.then_inc(s_dve, 1)
                dve.wait_ge(s_dve, steps[0])

            def rstd_of(norm, t):
                n = norm * TT + t
                c = slice(t, t + 1)
                dve.wait_ge(s_ss, n + 1)
                dve.tensor_scalar(var[:, c], ss[:, c], 1.0 / D, EPS, ALU.mult, ALU.add).then_inc(s_var, 1)
                dve.wait_ge(s_rs, n + 1)
                dve.tensor_tensor(tmp2[:, c], rstd[:, c], rstd[:, c], ALU.mult).then_inc(s_rr, 1)
                dve.wait_ge(s_rr, 4 * n + 1)
                dve.tensor_tensor(tmp2[:, c], tmp2[:, c], var[:, c], ALU.mult).then_inc(s_rr, 1)
                dve.wait_ge(s_rr, 4 * n + 2)
                dve.tensor_scalar(tmp2[:, c], tmp2[:, c], -0.5, 1.5, ALU.mult, ALU.add).then_inc(s_rr, 1)
                dve.wait_ge(s_rr, 4 * n + 3)
                dve.tensor_tensor(rstd[:, c], rstd[:, c], tmp2[:, c], ALU.mult).then_inc(s_rr, 1)
                dve.wait_ge(s_rr, 4 * n + 4)

            for t in range(TT):
                rstd_of(0, t)
                if t == 0:
                    dve.wait_ge(s_gmix, 16)
                dve.scalar_tensor_tensor(out=h_row[:, t, :], in0=xs[:, t, :], scalar=rstd[:, t:t + 1],
                                         in1=g_bc[:, :], op0=ALU.mult, op1=ALU.mult).then_inc(s_h, 1)
            dve.wait_ge(s_small_t, 1)
            link(dve.tensor_copy(cols[:, :], bank[4][:, 0:NCOLS]))
            for i in (1, 3):
                dve.wait_ge(s_tr, i + 1)
                dve.tensor_copy(h_t[:, 2 * i:2 * i + 2, :], bank[i][:, :].rearrange("p (a t) -> p a t", a=2)).then_inc(s_trD, 1)

            dve.wait_ge(s_gk, 1)
            for a in range(PAIRS):
                ins = dve.tensor_scalar(gk[:, a, :], bank[4][:, a * T:(a + 1) * T], cols[:, a:a + 1], None, ALU.add)
            ins.then_inc(s_gkb, 1)
            dve.wait_ge(s_const, 2)
            dve.wait_ge(s_ln, 1)
            link(dve.scalar_tensor_tensor(out=lb[:, :, :], in0=gk[:, :, :], scalar=0.0, in1=la[:, :, :],
                                          op0=ALU.min, op1=ALU.subtract))
            link(dve.tensor_copy(la[:, :, :], lb[:, :, :]))
            link(dve.tensor_tensor_scan(out=lb[:, :, :].rearrange("p a t -> p (a t)"),
                                        data0=reset[:, :, :].rearrange("p a t -> p (a t)"),
                                        data1=la[:, :, :].rearrange("p a t -> p (a t)"),
                                        initial=0.0, op0=ALU.mult, op1=ALU.add))
            lb_c = lb[:, :, :].rearrange("p a (n c) -> p (a n) c", c=CH)
            gk_c = gk[:, :, :].rearrange("p a (n c) -> p (a n) c", c=CH)
            dve.tensor_tensor(gk_c, lb_c[:, :, CH - 1:CH].broadcast_to([P, PAIRS * NCH, CH]), lb_c,
                              ALU.subtract).then_inc(s_cs, 1)
            dve.wait_ge(s_pk, 2)
            dve.wait_ge(s_ex, 1)
            dve.scalar_tensor_tensor(out=q_dec[:, :, :], in0=qk[:, 0, :, :], scalar=DK ** -0.5, in1=e_pos[:, :, :],
                                     op0=ALU.mult, op1=ALU.mult).then_inc(s_dec, 1)
            dve.wait_ge(s_ex, 2)
            for a in range(2):
                r = slice(DK * a, DK * (a + 1))
                dve.tensor_tensor(k_dec[r, :, a, :], qk[r, 1, :, :], e_neg[r, :, :], ALU.mult).then_inc(s_dec, 1)
            dve.wait_ge(s_ex, 3)
            dve.tensor_tensor(k_rem[:, :, :], qk[:, 1, :, :], e_rem[:, :, :], ALU.mult).then_inc(s_dec, 1)
            dve.wait_ge(s_kt, 1)
            dve.tensor_copy(k_row[:, :, :].rearrange("p t n -> p (t n)"), bank[5][:, :]).then_inc(s_krow, 1)

            def keep_scores(t):
                dve.wait_ge(s_sc, t + 1)
                src = bank[5 + t][:, :].rearrange("p (h c) -> p h c", h=HEADS)
                for a in range(2):
                    r = slice(CH * a, CH * (a + 1))
                    dve.tensor_copy(sc[r, t, :, r], src[r, :, r]).then_inc(s_sck, 1)

            for n in range(NCH - 1):
                dve.wait_ge(s_kv, n + 1)
                kv = bank[(6, 7, 4)[n]][:, :].rearrange("p (a b v) -> p a b v", a=PAIRS, b=2)
                for b in range(2):
                    r = slice(DK * b, DK * (b + 1))
                    if n == 0:
                        ins = dve.tensor_copy(state[r, 0, :, b, :], kv[r, :, b, :])
                    else:
                        for a in range(PAIRS):
                            last = (n + 1) * CH - 1
                            ins = dve.scalar_tensor_tensor(out=state[r, n, a, b, :], in0=state[r, n - 1, a, b, :],
                                                           scalar=e_pos[r, a, last:last + 1], in1=kv[r, a, b, :],
                                                           op0=ALU.mult, op1=ALU.add)
                ins.then_inc(s_st, 1)
                dve.wait_ge(s_st, n + 1)
            keep_scores(0)
            keep_scores(1)
            dve.wait_ge(s_sg, 1)
            link(dve.tensor_scalar(sil[:, :, :], sil[:, :, :], 1.0, None, ALU.add))
            link(dve.reciprocal(sil[:, :, :], sil[:, :, :]))
            link(dve.tensor_tensor(sil[:, :, :], sil[:, :, :], g_t[:, :, :], ALU.mult))
            link(dve.tensor_scalar(sil[:, :, :], sil[:, :, :], cols[:, 2:3], None, ALU.mult))

            for i in range(2):
                r = slice(2 * i, 2 * i + 2)
                dve.wait_ge(s_pk, 8 + i)
                dve.wait_ge(s_pj, 10 + i)
                link(dve.tensor_tensor(u_pad[:, r, TAPS - 1:], two_tiles(9 + i), u_t[:, r, :], ALU.mult))
                for j in range(TAPS):
                    for c in range(2 * i, 2 * i + 2):
                        w = cols[:, 3 + j * CT + c:4 + j * CT + c]
                        src = u_pad[:, c, j:j + T]
                        if j == 0:
                            ins = dve.tensor_scalar(conv[:, c, :], src, w, None, ALU.mult)
                        else:
                            ins = dve.scalar_tensor_tensor(out=conv[:, c, :], in0=src, scalar=w, in1=conv[:, c, :],
                                                           op0=ALU.mult, op1=ALU.add)
                    link(ins)
            for i in range(2):
                r = slice(2 * i, 2 * i + 2)
                dve.wait_ge(s_or, i + 1)
                link(dve.tensor_tensor(o_r[:, r, :], bank[(7, 4)[i]][:, :].rearrange("p (a t) -> p a t", a=2),
                                       o_r[:, r, :], ALU.mult))
                dve.tensor_tensor(y_t[:, CT + 2 * i:CT + 2 * i + 2, :], o_r[:, r, :], sil[:, r, :],
                                  ALU.mult).then_inc(s_ygla, 1)
            for i in range(2):
                r = slice(2 * i, 2 * i + 2)
                dve.wait_ge(s_pj, 12 + i)
                dve.tensor_tensor(y_t[:, r, :], two_tiles(11 + i), conv[:, r, :], ALU.mult).then_inc(s_yconv, 1)

            dve.wait_ge(s_late, 16 * 3)
            dve.tensor_tensor(wr_g[:, :, :], wr[:, :, :],
                              cols[:, FFN0:NCOLS].rearrange("p (k a) -> p k a", a=1).broadcast_to([P, KT, E]),
                              ALU.mult).then_inc(s_wr, 1)
            for t in range(TT):
                for n in range(2):
                    dve.wait_ge(s_op, 2 * t + n + 1)
                    dve.tensor_tensor(xs[:, t, n * 512:(n + 1) * 512], xs[:, t, n * 512:(n + 1) * 512],
                                      bank[OUT_BANK[2 * t + n]][:, :], ALU.add).then_inc(s_x2, 1)
            for t in range(TT):
                rstd_of(1, t)

            dve.wait_ge(s_lg, 1)
            for t in range(TT):
                ins = dve.scalar_tensor_tensor(out=lg[:, t, :], in0=bank[4][:, t * E:(t + 1) * E], scalar=rstd[:, t:t + 1],
                                               in1=br_bc[:, :], op0=ALU.mult, op1=ALU.add)
            link(ins)
            for t in range(TT):
                ins = dve.max(out=lmax[:, t, :], in_=lg[:, t, :])
            link(ins)
            dve.tensor_tensor(ex[:, :, :], lg[:, :, :], lmax[:, :, 0:1].broadcast_to([P, TT, E]),
                              ALU.subtract).then_inc(s_lgk, 1)
            fourth = lmax[:, :, TOP - 1:TOP].broadcast_to([P, TT, E])
            dve.tensor_tensor(gt[:, :, :], lg[:, :, :], fourth, ALU.is_gt)
            link(dve.tensor_tensor(eq[:, :, :], lg[:, :, :], fourth, ALU.is_equal))
            dve.tensor_reduce(ngt[:, :], gt[:, :, :], AX.X, ALU.add)
            for t in range(TT):
                ins = dve.tensor_tensor_scan(out=cum[:, t, :], data0=ones[:, 0:E], data1=eq[:, t, :], initial=0.0,
                                             op0=ALU.mult, op1=ALU.add)
            link(ins)
            for t in range(TT):
                ins = dve.tensor_scalar(cum[:, t, :], cum[:, t, :], ngt[:, t:t + 1], float(TOP), ALU.add, ALU.is_le)
            link(ins)
            link(dve.tensor_tensor(eq[:, :, :], eq[:, :, :], cum[:, :, :], ALU.mult))
            dve.tensor_tensor(chosen[:, :, :], eq[:, :, :], gt[:, :, :], ALU.add).then_inc(s_cho, 1)
            for t in range(TT):
                dve.scalar_tensor_tensor(out=h2[:, t, :], in0=xs[:, t, :], scalar=rstd[:, t:t + 1],
                                         in1=gffn_bc[:, :], op0=ALU.mult, op1=ALU.mult).then_inc(s_h2, 1)
            dve.wait_ge(s_cnt, 1)
            link(dve.tensor_copy(cnt[:, :], bank[5][0:E, 2 * E:2 * E + 1]))
            dve.tensor_scalar(more[:, :], block_c[:, :], cnt[:, 0:1], None, ALU.is_lt).then_inc(s_more, 1)
            link(dve.scalar_tensor_tensor(out=rank1[:, :, :], in0=bank[5][:, 0:TT * E].rearrange("p (t e) -> p t e", t=TT),
                                          scalar=1.0, in1=chosen[:, :, :], op0=ALU.add, op1=ALU.mult))
            dve.wait_ge(s_le, 1)
            link(dve.tensor_tensor(ex[:, :, :], ex[:, :, :], chosen[:, :, :], ALU.mult))
            link(dve.tensor_reduce(ngt[:, :], ex[:, :, :], AX.X, ALU.add))
            link(dve.reciprocal(ngt[:, :], ngt[:, :]))
            dve.tensor_tensor(gates[:, :, :], ex[:, :, :],
                              ngt[:, :].rearrange("p (t a) -> p t a", a=1).broadcast_to([P, TT, E]), ALU.mult).then_inc(s_gtk, 1)
            dve.wait_ge(s_gtk, 1)

            def place_slots(e, boff):
                for t in range(TT):
                    dve.tensor_scalar(p_row[:, t, :], slot1[:, :, :].rearrange("p b s -> p (b s)")[:, ds(boff, P)],
                                      rank1[:, t, ds(e, 1)], None, ALU.is_equal)
                dve.tensor_copy(gate_c[:, :], gates[:, :, ds(e, 1)].rearrange("p t e -> p (t e)")).then_inc(s_p, 1)

            def pick_bias(e):
                dve.tensor_copy(bias_e[:, :, :], bias_t[:, :, :, ds(e, 1)].rearrange("p a f e -> p a (f e)")).then_inc(s_be, 1)

            def low_gathered(it):
                dve.wait_ge(s_xh, it + 1)
                dve.tensor_tensor(x_sp[:, :, 1, :], bank[3][:, :].rearrange("p (k s) -> p k s", k=KT),
                                  x_sp[:, :, 0, :], ALU.subtract).then_inc(s_xs, 1)

            dve.wait_ge(s_const, 3)
            place_slots(0, 0)
            dve.wait_ge(s_pref, 1)
            link(dve.tensor_reduce(n_f[0:1, 0:1], bank[7][0:1, 64:64 + BLOCKS - 1], AX.X, ALU.add))
            dve.tensor_scalar(n_items[0:1, :], n_f[0:1, 0:1], float(E), None, ALU.add).then_inc(s_items, 1)
            dve.wait_ge(s_gt, 1)
            dve.tensor_copy(gates_t[:, :, :], bank[6][0:E, 0:T].rearrange("e (t p) -> e t p", t=TT)).then_inc(s_gtk, 1)
            low_gathered(0)
            link(dve.tensor_copy(place[:, :], bank[7][0:E, 0:BLOCKS - 1]))
            tot = BLOCKS - 1
            for b in range(1, BLOCKS - 1):
                for a in range(b):
                    link(dve.tensor_tensor(place[:, b:b + 1], place[:, b:b + 1], bank[7][0:E, tot + a:tot + a + 1], ALU.add))
            link(dve.scalar_tensor_tensor(out=place[:, :], in0=place[:, :], scalar=1.0, in1=more[:, :],
                                          op0=ALU.add, op1=ALU.mult))
            for b in range(BLOCKS - 1):
                ins = dve.tensor_scalar(hot[:, b, :], extra1[:, :], place[:, b:b + 1], None, ALU.is_equal)
            ins.then_inc(s_hot, 1)
            dve.wait_ge(s_tab, 1)
            for a in range(2):
                link(dve.tensor_copy(table_f[0:1, a * TABLE + E:a * TABLE + E + EXTRA], bank[1][0:1, a * EXTRA:(a + 1) * EXTRA]))
            dve.tensor_copy(table[0:1, :], table_f[0:1, :]).then_inc(s_table, 1)
            dve.wait_ge(s_table, 1)

            dve.sem_inc(s_mixed, 1)
            dve.wait_ge(s_items, 1)
            n = dve.value_load(n_items[0:1, 0:1], min_val=E, max_val=E + EXTRA)
            dve.wait_ge(s_btk, 1)
            pick_bias(0)
            dve.sem_inc(s_gur, 1)

            with dve.Fori(0, n) as it:
                def lo(u):
                    i = SPLIT.index(u)
                    dve.wait_ge(s_hi, it * len(SPLIT) + (i + 1))
                    dve.tensor_tensor(w_lo[:, i % BUFS, :], ring[:, item_slot(u // 4), (u % 4) * UNIT:(u % 4 + 1) * UNIT],
                                      w_hi[:, i % BUFS, :], ALU.subtract).then_inc(s_lo, 1)

                def biased(h):
                    dve.wait_ge(s_gu, it * 4 + (2 + 2 * h + 2))
                    if h == 0:
                        dve.wait_ge(s_be, it + 1)
                    dve.tensor_tensor(gu_b[:, :, :, :],
                                      bank[2][:, :].rearrange("p (a f s) -> p a f s", a=2, f=4),
                                      bias_e[:, :, 4 * h:4 * h + 4].rearrange("p a (f s) -> p a f s", s=1)
                                      .broadcast_to([P, 2, 4, SLOTS]), ALU.add).then_inc(s_gur, 1)

                def limited(h):
                    dve.wait_ge(s_gur, it * 2 + (h + 2))
                    dve.tensor_scalar(g_lim[:, :, :], gu_b[:, 0, :, :], LIMIT, None, ALU.min).then_inc(s_gl, 1)
                    dve.tensor_scalar(u_lim[:, :, :], gu_b[:, 1, :, :], LIMIT, -LIMIT, ALU.min, ALU.max).then_inc(s_ul, 1)

                def multiplied(h):
                    dve.wait_ge(s_ul, it * 2 + (h + 1))
                    dve.wait_ge(s_gl, it * 2 + (h + 1))
                    dve.scalar_tensor_tensor(out=u_lim[:, :, :], in0=u_lim[:, :, :], scalar=1.0,
                                             in1=g_lim[:, :, :], op0=ALU.add, op1=ALU.mult).then_inc(s_um, 1)

                def activated(h):
                    dve.wait_ge(s_sig, it * 2 + (h + 1))
                    dve.wait_ge(s_um, it * 2 + (h + 1))
                    dve.tensor_tensor(act[:, :, :], g_sig[:, :, :], u_lim[:, :, :], ALU.mult).then_inc(s_av, 1)

                def low_activated(h):
                    dve.wait_ge(s_ah, it * 2 + (h + 1))
                    dve.tensor_tensor(a_sp[:, 4 * h:4 * h + 4, 1, :], act[:, :, :], a_sp[:, 4 * h:4 * h + 4, 0, :],
                                      ALU.subtract).then_inc(s_a, 1)

                e_next = dve.value_load(table[0:1, ds(it + 1, 1)], min_val=0, max_val=E - 1)
                b_next = dve.value_load(table[0:1, ds(it + (TABLE + 1), 1)], min_val=0, max_val=(BLOCKS - 1) * P)
                for u in range(2, 8):
                    lo(u)
                dve.wait_ge(s_pt, it + 1)
                place_slots(e_next, b_next)
                for u in range(8, 13):
                    lo(u)
                biased(0)
                lo(13)
                limited(0)
                multiplied(0)
                lo(14)
                activated(0)
                lo(15)
                low_activated(0)
                lo(16)
                lo(17)
                lo(20)
                biased(1)
                limited(1)
                multiplied(1)
                activated(1)
                lo(21)
                low_activated(1)
                lo(22)
                lo(23)
                pick_bias(e_next)
                for i, nn in enumerate((1, 0)):
                    dve.wait_ge(s_zh, it * 2 + (i + 1))
                    dve.scalar_tensor_tensor(out=z_lo[:, nn * 512:(nn + 1) * 512], in0=bank[nn][:, :],
                                             scalar=gate_s[:, 0:1], in1=z_hi[:, nn * 512:(nn + 1) * 512],
                                             op0=ALU.mult, op1=ALU.subtract).then_inc(s_zl, 1)
                low_gathered(it + 1)

            dve.wait_ge(s_y, n)
            for t in range(TT):
                for nn in range(2):
                    c = slice(nn * 512, (nn + 1) * 512)
                    dve.tensor_tensor(xs[:, t, c], xs[:, t, c], y_ps[t][nn][:, :], ALU.add).then_inc(s_x3, 1)
            for t in range(TT):
                rstd_of(2, t)
                if t == 0:
                    dve.wait_ge(s_gfin, 16)
                dve.scalar_tensor_tensor(out=y_out[:, t, :], in0=xs[:, t, :], scalar=rstd[:, t:t + 1],
                                         in1=g_bc[:, :], op0=ALU.mult, op1=ALU.mult).then_inc(s_fin, 1)

        @block.tensor
        def _(pe):
            mm = nc.tensor.matmul

            pe.wait_ge(s_const, 1)
            pe.wait_ge(s_small, 16 * 8)
            nc.tensor.transpose(bank[4][:, 0:NCOLS], rows[:, :], ident[0:NCOLS, 0:NCOLS]).then_inc(s_small_t, 1)

            for i in range(4):
                for k in range(2):
                    for t in range(TT):
                        if i == 0 and k == 0:
                            pe.wait_ge(s_h, t + 1)
                        ins = nc.tensor.transpose(bank[i][:, k * T + t * P:k * T + (t + 1) * P],
                                                  h_row[:, t, (2 * i + k) * P:(2 * i + k + 1) * P], ident[:, :])
                ins.then_inc(s_tr, 1)
            pe.wait_ge(s_trA, 2)
            pe.wait_ge(s_trD, 2)

            def project(n):
                what, i = PROJ[n]
                dst = bank[n % 4]
                if n >= 4:
                    pe.wait_ge(s_pk, n - 3)
                if what == "gk":
                    for k in range(KT):
                        ins = mm(dst[0:RANK, 0:T], wgk[:, k, :], h_t[:, k, :], start=k == 0, stop=k == KT - 1)
                    ins.then_inc(s_pj, 1)
                    return
                if i == 0:
                    pe.wait_ge(s_slot[slot_of(what)], 16)
                w = chunk_view(what, KT)
                if what == VV:
                    for k in range(KT):
                        ins = mm(dst[:, :], h_t[:, k, i * P:(i + 1) * P], w[:, k, :], start=k == 0, stop=k == KT - 1)
                else:
                    for m in range(2):
                        for k in range(KT):
                            ins = mm(dst[:, m * T:(m + 1) * T], w[:, k, (2 * i + m) * P:(2 * i + m + 1) * P],
                                     h_t[:, k, :], start=k == 0, stop=k == KT - 1)
                ins.then_inc(s_pj, 1)
                if i == 1:
                    pe.wait_ge(s_pj, n + 1)
                    pe.sem_inc(s_used, 1)

            for n in range(3):
                project(n)
            pe.wait_ge(s_pk, 3)
            pe.wait_ge(s_trD, 2)
            for a in range(PAIRS):
                ins = mm(bank[4][:, a * T:(a + 1) * T], wgu[:, a, :], gkl[:, :], start=True, stop=True)
            ins.then_inc(s_gk, 1)
            project(3)
            project(4)
            pe.wait_ge(s_dec, 4)
            for t in range(TT):
                for a in range(PAIRS):
                    ins = nc.tensor.transpose(bank[5][:, (t * PAIRS + a) * P:(t * PAIRS + a + 1) * P],
                                              k_rem[:, a, t * P:(t + 1) * P], ident[:, :])
            ins.then_inc(s_kt, 1)
            project(5)
            project(6)
            pe.wait_ge(s_krow, 1)
            pe.wait_ge(s_pk, 5)
            for n in range(NCH - 1):
                r = slice(CH * (n % 2), CH * (n % 2 + 1))
                for a in range(PAIRS):
                    ins = mm(bank[(6, 7, 4)[n]][:, a * 2 * DV:(a + 1) * 2 * DV], k_row[r, n // 2, a * P:(a + 1) * P],
                             v_row[r, n // 2, a * 2 * DV:(a + 1) * 2 * DV], start=True, stop=True)
                ins.then_inc(s_kv, 1)
            for t in range(TT):
                if t == 1:
                    pe.wait_ge(s_st, 1)
                for h in range(HEADS):
                    ins = mm(bank[5 + t][:, h * P:(h + 1) * P], k_dec[:, h // 2, h % 2, t * P:(t + 1) * P],
                             q_dec[:, h // 2, t * P:(t + 1) * P], start=True, stop=True)
                ins.then_inc(s_sc, 1)
            project(7)
            project(8)
            pe.wait_ge(s_mask, 2)
            pe.wait_ge(s_st, 3)
            for i in range(2):
                dst = bank[(7, 4)[i]]
                for h in range(2 * i, 2 * i + 2):
                    for t in range(TT):
                        c0 = (h % 2) * T + t * P
                        mm(dst[:, c0:c0 + P], v_row[:, t, h * DV:(h + 1) * DV], sc[:, t, h, :], start=True, stop=False)
                        for n in range(2 * t, 2 * t + 2):
                            if n == 0:
                                continue
                            c1 = c0 + CH * (n % 2)
                            ins = mm(dst[:, c1:c1 + CH], state[:, n - 1, h // 2, h % 2, :],
                                     q_dec[:, h // 2, n * CH:(n + 1) * CH], start=False, stop=n % 2 == 1)
                ins.then_inc(s_o, 1)
            project(9)
            project(10)
            for i in range(2):
                pe.wait_ge(s_osq, i + 1)
                pe.wait_ge(s_sck, 2 * (i + 1))
                mm(bank[5 + i][:, :], ones[:, :], o_sq[:, 2 * i:2 * i + 2, :].rearrange("p a t -> p (a t)"),
                   start=True, stop=True).then_inc(s_ms, 1)
            project(11)
            project(12)
            pe.wait_ge(s_ygla, 2)
            for t in range(TT):
                for n in range(2):
                    w = chunk_view(WO + n, KT)
                    if t == 0:
                        pe.wait_ge(s_slot[slot_of(WO + n)], 32)
                    for j, k in enumerate(list(range(CT, KT)) + list(range(CT))):
                        if t == 0 and n == 0 and k in (0, 2):
                            pe.wait_ge(s_yconv, k // 2 + 1)
                        ins = mm(bank[OUT_BANK[2 * t + n]][:, :], y_t[:, k, t * P:(t + 1) * P], w[:, k, :],
                                 start=j == 0, stop=j == KT - 1)
                    ins.then_inc(s_op, 1)
            pe.wait_ge(s_op, 4)
            pe.sem_inc(s_used, 2)
            pe.wait_ge(s_wr, 1)
            for t in range(TT):
                pe.wait_ge(s_x2, 2 * (t + 1))
                if t > 0:
                    pe.wait_ge(s_trA, 4)
                for i in range(2):
                    for k in range(4):
                        ins = nc.tensor.transpose(bank[(0, 3)[i]][:, k * P:(k + 1) * P],
                                                  xs[:, t, (4 * i + k) * P:(4 * i + k + 1) * P], ident[:, :])
                    ins.then_inc(s_tr, 1)
                pe.wait_ge(s_trA, 2 + 2 * (t + 1))
                for k in range(KT):
                    ins = mm(bank[4][:, t * E:(t + 1) * E], h_t[:, k, t * P:(t + 1) * P], wr_g[:, k, :],
                             start=k == 0, stop=k == KT - 1)
            ins.then_inc(s_lg, 1)
            pe.wait_ge(s_cho, 1)
            pe.wait_ge(s_const, 3)
            mm(bank[5][:, 0:E], before[:, :], chosen[:, 0, :], start=True, stop=True)
            mm(bank[5][:, E:2 * E], before[:, :], chosen[:, 1, :], start=True, stop=False)
            mm(bank[5][:, E:2 * E], ones[:, :], chosen[:, 0, :], start=False, stop=True)
            for t in range(TT):
                ins = mm(bank[5][0:E, 2 * E:2 * E + 1], chosen[:, t, :], ones[:, 0:1], start=t == 0, stop=t == TT - 1)
            ins.then_inc(s_cnt, 1)
            pe.wait_ge(s_more, 1)
            nb = BLOCKS - 1
            mm(bank[7][0:E, 0:nb], before[0:E, 0:E], more[:, :], start=True, stop=True)
            mm(bank[7][0:E, nb:2 * nb], ones[0:E, 0:E], more[:, :], start=True, stop=True)
            mm(bank[7][0:1, 64:64 + nb], ones[0:E, 0:1], more[:, :], start=True, stop=True).then_inc(s_pref, 1)
            pe.wait_ge(s_gtk, 1)
            for t in range(TT):
                ins = nc.tensor.transpose(bank[6][0:E, t * P:(t + 1) * P], gates[:, t, :], ident[:, :])
            ins.then_inc(s_gt, 1)

            def gather(it):
                for k in range(KT):
                    for t in range(TT):
                        ins = mm(bank[3][:, k * SLOTS:(k + 1) * SLOTS], h2[:, t, k * P:(k + 1) * P],
                                 p_row[:, t, 0:SLOTS].bitcast(f32), start=t == 0, stop=t == TT - 1)
                ins.then_inc(s_xg, 1)

            pe.wait_ge(s_h2, 2)
            pe.wait_ge(s_p, 1)
            gather(0)
            pe.wait_ge(s_hot, 1)
            for a in range(2):
                for b in range(nb):
                    ins = mm(bank[1][0:1, a * EXTRA:(a + 1) * EXTRA],
                             exp_c[:, 0:1] if a == 0 else boff_c[:, b:b + 1], hot[:, b, :],
                             start=b == 0, stop=b == nb - 1)
            ins.then_inc(s_tab, 1)
            pe.wait_ge(s_bias, 32)
            for i in range(2 * F // P):
                ins = nc.tensor.transpose(bank[2][:, i * E:(i + 1) * E], bgu[:, i * P:(i + 1) * P], ident[0:E, 0:E])
            ins.then_inc(s_bt, 1)
            pe.wait_ge(s_gtk, 2)
            pe.wait_ge(s_hot, 1)
            for t in range(TT):
                for nn in range(2):
                    ins = mm(y_ps[t][nn][:, :], gates_t[:, t, :], bdn[:, nn * 512:(nn + 1) * 512], start=True, stop=True)
            ins.then_inc(s_mixed, 1)
            pe.wait_ge(s_table, 1)
            pe.wait_ge(s_btk, 1)
            n = pe.value_load(n_items[0:1, 0:1], min_val=E, max_val=E + EXTRA)
            pe.sem_inc(s_free, AHEAD)
            pe.sem_inc(s_gu, 2)

            with pe.Fori(0, n) as it:
                def unit(u, last=False, between=None):
                    j, uu = u // 4, u % 4
                    slot = ring[:, item_slot(j), uu * UNIT:(uu + 1) * UNIT]
                    if u in WHOLE:
                        if uu == 0:
                            pe.wait_ge(s_slot[item_slot(j)], item_loaded(it, j))
                        parts = [slot]
                    else:
                        i = SPLIT.index(u)
                        pe.wait_ge(s_lo, it * len(SPLIT) + (i + 1))
                        parts = [w_hi[:, i % BUFS, :], w_lo[:, i % BUFS, :]]
                    whole = u in WHOLE

                    def stationary(ap):
                        return ap.bitcast(f32) if whole else ap

                    if j < 4:
                        for kk in range(2):
                            k = 2 * uu + kk
                            lhs = stationary(x_sp[:, k, :, :].rearrange("p a s -> p (a s)"))
                            for q, w in enumerate(parts):
                                ins = mm(bank[j % 2][:, :], lhs, w[:, kk * 512:(kk + 1) * 512],
                                         start=k == 0 and q == 0, stop=k == KT - 1 and q == len(parts) - 1)
                    else:
                        k = 4 * (j - 4) + uu
                        lhs = stationary(a_sp[:, k, :, :].rearrange("p a s -> p (a s)"))
                        for nn in (0, 1) if between else (1, 0):
                            for q, w in enumerate(parts):
                                ins = mm(bank[nn][:, :], lhs, w[:, nn * 512:(nn + 1) * 512],
                                         start=k == 0 and q == 0, stop=k == KT - 1 and q == len(parts) - 1)
                            if k == KT - 1 and nn == 1:
                                ins.then_inc(s_dn, 1)
                            if between and nn == 0:
                                between()
                    if last:
                        ins.then_inc(s_used, 1)
                    elif not whole:
                        ins.then_inc(s_free, 1)

                def chunk(j):
                    for uu in range(4):
                        unit(4 * j + uu, last=uu == 3)

                def fold_up(c):
                    pe.wait_ge(s_up, it * 4 + (c + 1))
                    if c % 2 == 0:
                        pe.wait_ge(s_gur, it * 2 + (c // 2 + 1))
                    for f in range(4):
                        o = (c % 2) * 4 * SLOTS + f * SLOTS
                        ins = mm(bank[2][:, o:o + SLOTS], up_sb[:, c % 2, f * P:(f + 1) * P], fold[:, :],
                                 start=True, stop=True)
                    ins.then_inc(s_gu, 1)

                pe.wait_ge(s_xs, it + 1)
                chunk(0)
                for t in range(TT):
                    nc.tensor.transpose(bank[3][:, t * P:(t + 1) * P], p_row[:, t, :].bitcast(f32), ident[:, :])
                for t in range(TT):
                    ins = mm(bank[3][:, T:T + 1], p_row[:, t, :].bitcast(f32), gate_c[:, t:t + 1],
                             start=t == 0, stop=t == TT - 1)
                ins.then_inc(s_pt, 1)
                unit(4)
                unit(5)
                fold_up(0)
                unit(6)
                unit(7, last=True)
                unit(8)
                unit(9)
                fold_up(1)
                unit(10)
                unit(11, last=True)
                unit(12)
                unit(13)
                fold_up(2)
                unit(14)
                unit(15, last=True)
                pe.wait_ge(s_a, it * 2 + 1)
                unit(16, between=lambda: fold_up(3))
                unit(17)
                unit(18)
                unit(19, last=True)
                pe.wait_ge(s_a, it * 2 + 2)
                chunk(5)
                pe.wait_ge(s_p, it + 2)
                pe.wait_ge(s_ptk, it + 1)
                gather(it + 1)
                for i, nn in enumerate((1, 0)):
                    pe.wait_ge(s_zl, it * 2 + (i + 1))
                    for t in range(TT):
                        for q, z in enumerate((z_hi, z_lo)):
                            ins = mm(y_ps[t][nn][:, :], p_t[:, t * P:(t + 1) * P], z[:, nn * 512:(nn + 1) * 512],
                                     start=False, stop=False, skip_group_check=True)
                ins.then_inc(s_y, 1)


_INS = ["x", "norm_mix_g", "w_in", "conv_w", "w_gk_up", "b_gk_up", "gla_norm_g", "w_out", "norm_ffn_g",
        "w_router", "b_router", "w_gate_up", "b_gate_up", "w_down", "b_down", "norm_final_g"]


def kernel(**inputs):
    import numpy as _np
    import concourse.bacc as _bacc
    from concourse import mybir as _mybir
    from concourse.bass_utils import run_bass_kernel_spmd as _run

    nc = _bacc.Bacc("TRN2", target_bir_lowering=False, num_devices=1)
    arrays, args = {}, []
    for name in _INS:
        a = _np.ascontiguousarray(inputs[name])
        arrays[f"in_{name}"] = a
        args.append(nc.dram_tensor(f"in_{name}", a.shape, _mybir.dt.from_np(a.dtype), kind="ExternalInput").ap())
    args.append(nc.dram_tensor("out", (1, T, D), _mybir.dt.float32, kind="ExternalOutput").ap())
    build(nc, *args)
    r = _run(nc, [arrays], core_ids=[0])
    return r.results[0]["out"]
```

```python
import numpy as np
import concourse.bass as bass
from concourse import mybir
from contextlib import ExitStack

P = 128
D = 1024
T = 256
TT = T // P
KT = D // P
CONV = 512
CT = CONV // P
TAPS = 3
HEADS = 4
DK = 64
DV = 128
PAIRS = HEADS // 2
CH = 64
NCH = T // CH
RANK = 16
NORMALIZER = 16.0
E = 32
TOP = 4
F = 1024
LIMIT = 7.0
ALPHA = 1.702
EPS = 1e-5
SLOTS = 64
BLOCKS = T // SLOTS
EXTRA = T * TOP // SLOTS
TABLE = E + 2 * EXTRA
SPLITS = P // E
assert SPLITS == 4
NCOLS = 2 + 1 + TAPS * CT + KT
FFN0 = 2 + 1 + TAPS * CT

CHUNK = 4096
RING = 6
MIX_CHUNKS = 8
QK, VV, GG, UU, CC, BB, WO = range(7)
ITEM_CHUNKS = 6
UNIT = 1024
UNITS = ITEM_CHUNKS * CHUNK // UNIT
WHOLE = (7, 12, 16, 18)
SPLIT = [u for u in range(UNITS) if u not in WHOLE]
BUFS = 4
assert len(SPLIT) % BUFS == 0
FREED = [u for u in SPLIT if u % 4 != 3]
AHEAD = sum(u % 4 != 3 for u in SPLIT[-BUFS:])


def slot_of(chunk):
    return chunk % RING


def build(nc, x, norm_mix_g, w_in, conv_w, w_gk_up, b_gk_up, gla_norm_g, w_out, norm_ffn_g,
          w_router, b_router, w_gate_up, b_gate_up, w_down, b_down, norm_final_g, out):
    f32 = mybir.dt.float32
    f32r = mybir.dt.float32r
    i32 = mybir.dt.int32
    ALU = mybir.AluOpType
    ACT = mybir.ActivationFunctionType
    AX = mybir.AxisListType
    ds = bass.ds

    x_v = x[0].rearrange("(t p) d -> p t d", p=P)
    out_v = out[0].rearrange("(t p) d -> p t d", p=P)
    win_v = w_in[0].rearrange("(k p) n -> p k n", p=P)
    wout_v = w_out[0].rearrange("(k p) n -> p k n", p=P)
    wr_v = w_router[0].rearrange("(k p) n -> p k n", p=P)
    gu_v = w_gate_up[0].rearrange("e (k p) n -> p e k n", p=P)
    dn_v = w_down[0].rearrange("e (k p) n -> p e k n", p=P)
    col0 = {UU: 0, BB: CONV, CC: 2 * CONV, QK: 3 * CONV, VV: 4 * CONV, GG: 5 * CONV}
    GKLOW0 = 6 * CONV

    ctx = ExitStack()
    with ctx:
        def sb(name, shape, dt=f32, scope=ctx):
            return scope.enter_context(nc.sbuf_tensor(name, shape, dt))

        def sem(name):
            return ctx.enter_context(nc.semaphore(name))

        ring = sb("ring", [P, RING, CHUNK])
        xs = sb("x_sb", [P, TT, D])
        g_bc = sb("g_bc", [P, D])
        ident = sb("ident", [P, P])
        ones = sb("ones", [P, P])
        before = sb("before", [P, P])
        fold = sb("fold", [P, SLOTS])
        slot1 = sb("slot1", [P, BLOCKS, P])
        eps_c = sb("eps_c", [P, 1])
        one_c = sb("one_c", [P, 1])
        ss = sb("ss", [P, TT])
        var = sb("var", [P, TT])
        lnv = sb("lnv", [P, TT])
        rstd = sb("rstd", [P, TT])
        tmp2 = sb("tmp2", [P, TT])
        gates = sb("gates", [P, TT, E])
        rank1 = sb("rank1", [P, TT, E])
        bias_t = sb("bias_t", [P, 2, F // P, E])
        bias_e = sb("bias_e", [P, 2, F // P])
        table = sb("table", [1, 2 * TABLE], i32)
        n_items = sb("n_items", [1, 2], i32)

        router = ExitStack()
        mixer = ExitStack()
        late = ExitStack()

        def rb(name, shape, dt=f32):
            return sb(name, shape, dt, router)

        h_t = rb("h_t", [P, KT, T])
        h_row = rb("h_row", [P, TT, D])
        y_t = h_row[:, :, :].rearrange("p t (k n) -> p (t k) n", n=T)
        gffn_bc = rb("gffn_bc", [P, D])
        wr = rb("wr", [P, KT, E])
        wr_g = rb("wr_g", [P, KT, E])
        br_bc = rb("br_bc", [P, E])
        lg = rb("lg", [P, TT, E])
        lmax = rb("lmax", [P, TT, 8])
        ngt = rb("ngt", [P, TT])
        gt = rb("gt", [P, TT, E])
        eq = rb("eq", [P, TT, E])
        cum = rb("cum", [P, TT, E])
        chosen = rb("chosen", [P, TT, E])
        ex = rb("ex", [P, TT, E])
        gates4 = rb("gates4", [P, TT, SPLITS, E])
        gates_t = rb("gates_t", [P, TT, P], f32r)
        cnt = rb("cnt", [E, 1])
        more = rb("more", [E, BLOCKS - 1])
        block_c = rb("block_c", [E, BLOCKS - 1])
        boff_c = rb("boff_c", [E, BLOCKS - 1])
        exp_c = rb("exp_c", [E, 1])
        place = rb("place", [E, BLOCKS - 1])
        extra1 = rb("extra1", [E, EXTRA])
        hot = rb("hot", [E, BLOCKS - 1, EXTRA])
        table_f = rb("table_f", [1, 2 * TABLE])
        n_f = rb("n_f", [1, BLOCKS - 1])

        def mb(name, shape, dt=f32):
            return sb(name, shape, dt, mixer)

        wgk = mb("wgk", [P, KT, RANK])
        wgu = mb("wgu", [RANK, PAIRS, P])
        rows = mb("rows", [NCOLS, P])
        cols = mb("cols", [P, NCOLS])
        gmix_row = mb("gmix_row", [KT, P])
        gmix_c = mb("gmix_c", [P, KT])
        gkl = mb("gkl", [RANK, T])
        gk = mb("gk", [P, PAIRS, T])
        la = mb("la", [P, PAIRS, T])
        lb = mb("lb", [P, PAIRS, T])
        e_pos = mb("e_pos", [P, PAIRS, T])
        e_neg = mb("e_neg", [P, PAIRS, T])
        e_rem = mb("e_rem", [P, PAIRS, T])
        qk = mb("qk", [P, 2, PAIRS, T])
        o_r = qk[:, :, :, :].rearrange("p a b t -> p (a b) t")
        q_dec = mb("q_dec", [P, PAIRS, T])
        k_dec = mb("k_dec", [P, PAIRS, 2, T])
        o_sq = k_dec[:, :, :, :].rearrange("p a b t -> p (a b) t")
        k_rem = mb("k_rem", [P, PAIRS, T])
        k_row = mb("k_row", [P, TT, PAIRS * P])
        v_row = mb("v_row", [P, TT, HEADS * DV])
        g_t = mb("g_t", [P, HEADS, T])
        sil = mb("sil", [P, HEADS, T])
        state = mb("state", [P, NCH - 1, PAIRS, 2, DV])
        sc = mb("sc", [P, TT, HEADS, P])
        reset = mb("reset", [P, PAIRS * NCH, CH])
        u_t = mb("u_t", [P, CT, T])
        u_pad = mb("u_pad", [P, CT, T + TAPS - 1])
        conv = mb("conv", [P, CT, T])
        mixer.close()

        bgu = sb("bgu", [E, 2 * F], f32, late)
        bdn = sb("bdn", [P, D], f32, late)
        late.close()
        router.close()

        w_hi = sb("w_hi", [P, BUFS, UNIT], f32r)
        w_lo = sb("w_lo", [P, BUFS, UNIT], f32r)
        z_hi = sb("z_hi", [P, D], f32r)
        z_lo = sb("z_lo", [P, D], f32r)
        h2 = sb("h2", [P, TT, D])
        x_sp = sb("x_sp", [P, KT, 2, SLOTS], f32r)
        p_row = sb("p_row", [P, TT, P], f32r)
        gate_c = sb("gate_c", [P, TT])
        up_sb = sb("up_sb", [P, 2, 512])
        gu_b = sb("gu_b", [P, 2, 4, SLOTS])
        g_lim = sb("g_lim", [P, 4, SLOTS])
        u_lim = sb("u_lim", [P, 4, SLOTS])
        g_sig = sb("g_sig", [P, 4, SLOTS])
        act = sb("act", [P, 4, SLOTS])
        a_sp = sb("a_sp", [P, F // P, 2, SLOTS], f32r)
        p_t = sb("p_t", [P, T], f32r)
        gate_s = sb("gate_s", [P, 1])
        start = ExitStack()
        bdn_sp = sb("bdn_sp", [P, D], f32r, start)
        start.close()
        y_out = sb("y_out", [P, TT, D])

        bank = [ctx.enter_context(nc.psum_tensor(f"bank{i}", [P, 512], f32)) for i in range(8)]
        y_ps = [[bank[4 + 2 * t + n] for n in range(2)] for t in range(TT)]

        s_x = [sem(f"x{t}_loaded") for t in range(TT)]
        s_gmix = sem("g_mix_loaded")
        s_small = sem("small_loaded")
        s_late = sem("router_weights_loaded")
        s_bias = sem("expert_biases_loaded")
        s_gfin = sem("g_final_loaded")
        s_slot = [sem(f"slot{i}_loaded") for i in range(RING)]
        s_used = sem("chunk_used")
        s_const = sem("consts_ready")
        s_ss = sem("squares_summed")
        s_var = sem("variance_ready")
        s_rs = sem("rsqrt_ready")
        s_lv = sem("log_variance_ready")
        s_sp = sem("softplus_step")
        s_ol = sem("o_log_ready")
        s_rr = sem("rsqrt_refined")
        s_wr = sem("router_weights_scaled")
        s_h = sem("h_ready")
        s_tr = sem("transposed")
        s_trA = sem("transposed_kept_act")
        s_trD = sem("transposed_kept_dve")
        s_small_t = sem("small_transposed")
        s_cols = sem("cols_ready")
        s_pj = sem("projected")
        s_pk = sem("projection_kept")
        s_gk = sem("gk_ready")
        s_gkb = sem("gk_biased")
        s_ln = sem("softplus_ready")
        s_cs = sem("log_sums_ready")
        s_ex = sem("decays_ready")
        s_dec = sem("decayed_ready")
        s_kt = sem("k_transposed")
        s_krow = sem("k_row_ready")
        s_kv = sem("kv_ready")
        s_st = sem("state_ready")
        s_sc = sem("scores_ready")
        s_sck = sem("scores_kept")
        s_mask = sem("scores_masked")
        s_o = sem("o_ready")
        s_osq = sem("o_squared")
        s_ms = sem("o_mean_ready")
        s_or = sem("o_rsqrt_ready")
        s_sg = sem("silu_exp_ready")
        s_ygla = sem("y_gla_ready")
        s_yconv = sem("y_conv_ready")
        s_op = sem("out_projected")
        s_x2 = sem("x2_ready")
        s_h2 = sem("h2_ready")
        s_bt = sem("bias_transposed")
        s_btk = sem("bias_t_ready")
        s_lg = sem("logits_ready")
        s_lgk = sem("logits_less_max")
        s_le = sem("logits_exp")
        s_cho = sem("chosen_ready")
        s_bh = sem("b_down_high_ready")
        s_bl = sem("b_down_split")
        s_cnt = sem("counted")
        s_more = sem("more_ready")
        s_pref = sem("prefix_ready")
        s_hot = sem("hot_ready")
        s_tab = sem("table_summed")
        s_items = sem("items_ready")
        s_table = sem("table_ready")
        s_be = sem("bias_picked")
        s_gt = sem("gates_transposed")
        s_gtk = sem("gates_t_ready")
        s_mixed = sem("router_space_free")
        s_free = sem("split_buffer_free")
        s_hi = sem("w_hi_ready")
        s_lo = sem("w_lo_ready")
        s_p = sem("p_row_ready")
        s_xg = sem("x_gathered")
        s_xh = sem("x_high_ready")
        s_xs = sem("x_split")
        s_pt = sem("p_transposed")
        s_ptk = sem("p_t_ready")
        s_up = sem("up_kept")
        s_gu = sem("gate_up_folded")
        s_gur = sem("gate_up_biased")
        s_gl = sem("gate_limited")
        s_ul = sem("up_limited")
        s_um = sem("up_times_gate")
        s_sig = sem("sigmoid_ready")
        s_av = sem("activation_ready")
        s_ah = sem("activation_high_ready")
        s_a = sem("activation_split")
        s_dn = sem("down_first_ready")
        s_zh = sem("z_hi_ready")
        s_zl = sem("z_lo_ready")
        s_y = sem("item_added")
        s_x3 = sem("x3_ready")
        s_fin = sem("out_ready")
        s_out = sem("out_stored")
        s_dve = sem("dve_step")
        s_pool = sem("pool_step")

        PROJ = [(QK, 0), (QK, 1), ("gk", 0), (VV, 0), (VV, 1), (GG, 0), (GG, 1),
                (UU, 0), (UU, 1), (CC, 0), (CC, 1), (BB, 0), (BB, 1)]
        OUT_BANK = (5, 6, 1, 2)

        def two_tiles(n):
            return bank[n % 4][:, :].rearrange("p (a t) -> p a t", a=2)

        def chunk_view(c, k):
            return ring[:, slot_of(c), :].rearrange("p (k n) -> p k n", k=k)

        def item_slot(j):
            return slot_of(MIX_CHUNKS + j)

        def item_loaded(it, j):
            return (it + (MIX_CHUNKS + j) // RING + 1) * 16

        block = ctx.enter_context(nc.Block())

        @block.sync
        def _(sp):
            for t in range(TT):
                sp.dma_start(xs[:, t, :], x_v[:, t, :]).then_inc(s_x[t], 16)
            sp.dma_start(rows[0:2, :], b_gk_up[0].rearrange("(a p) -> a p", p=P)).then_inc(s_small, 16)
            sp.dma_start(rows[2:3, :], gla_norm_g).then_inc(s_small, 16)
            for i in range(TAPS):
                sp.dma_start(rows[3 + i * CT:3 + (i + 1) * CT, :],
                                conv_w[0, i].rearrange("(a p) -> a p", p=P)).then_inc(s_small, 16)
            sp.dma_start(rows[FFN0:NCOLS, :], norm_ffn_g[0].rearrange("(a p) -> a p", p=P)).then_inc(s_small, 16)
            sp.dma_start(wgu[:, :, :], w_gk_up[0].rearrange("r (a p) -> r a p", p=P)).then_inc(s_small, 16)
            for c in range(MIX_CHUNKS):
                if c >= RING:
                    sp.wait_ge(s_used, c - RING + 1)
                if c < WO:
                    src = win_v[:, :, col0[c]:col0[c] + 512]
                else:
                    src = wout_v[:, :, (c - WO) * 512:(c - WO + 1) * 512]
                sp.dma_start(chunk_view(c, KT), src).then_inc(s_slot[slot_of(c)], 16)

            def load_item(it, e):
                for j in range(ITEM_CHUNKS):
                    sp.wait_ge(s_used, it * ITEM_CHUNKS + (MIX_CHUNKS + j - RING + 1))
                    if j < 4:
                        c0 = (j % 2) * F + (j // 2) * 512
                        src = gu_v[:, ds(e, 1), :, c0:c0 + 512].rearrange("p e k n -> p (e k) n")
                        dst = ring[:, item_slot(j), :].rearrange("p (k n) -> p k n", k=KT)
                    else:
                        src = dn_v[:, ds(e, 1), 4 * (j - 4):4 * (j - 3), :].rearrange("p e k n -> p (e k) n")
                        dst = ring[:, item_slot(j), :].rearrange("p (k n) -> p k n", k=4)
                    sp.dma_start(dst, src).then_inc(s_slot[item_slot(j)], 16)

            with sp.Fori(0, E) as it:
                load_item(it, it)
            sp.wait_ge(s_items, 1)
            n = sp.value_load(n_items[0:1, 0:1], min_val=E, max_val=E + EXTRA)
            with sp.If(n > E):
                with sp.Fori(E, n) as it:
                    sp.wait_ge(s_table, 1)
                    e = sp.value_load(table[0:1, ds(it, 1)], min_val=0, max_val=E - 1)
                    load_item(it, e)
            for t in range(TT):
                sp.wait_ge(s_fin, t + 1)
                sp.dma_start(out_v[:, t, :], y_out[:, t, :]).then_inc(s_out, 16)
            sp.wait_ge(s_out, 16 * TT)

        @block.gpsimd
        def _(pool):
            steps = [0]

            def link(ins):
                steps[0] += 1
                ins.then_inc(s_pool, 1)
                pool.wait_ge(s_pool, steps[0])

            link(pool.memset(ident[:, :], 0.0))
            link(pool.affine_select(out=ident[:, :], in_=ident[:, :], compare_op=ALU.not_equal, fill=1.0,
                                    base=0, pattern=[[-1, P]], channel_multiplier=1))
            link(pool.memset(ones[:, :], 1.0))
            link(pool.memset(eps_c[:, :], EPS))
            pool.memset(one_c[:, :], 1.0).then_inc(s_const, 1)
            link(pool.memset(k_dec[:, :, :, :], 0.0))
            link(pool.memset(u_pad[:, :, 0:TAPS - 1], 0.0))
            link(pool.memset(state[:, :, :, :, :], 0.0))
            link(pool.memset(sc[:, :, :, :], 0.0))
            link(pool.memset(reset[:, :, :], 1.0))
            pool.affine_select(out=reset[:, :, :], in_=reset[:, :, :], compare_op=ALU.is_gt, fill=0.0,
                               base=0, pattern=[[0, PAIRS * NCH], [1, CH]], channel_multiplier=0).then_inc(s_const, 1)
            link(pool.affine_select(out=before[:, :], in_=ones[:, :], compare_op=ALU.is_gt, fill=0.0,
                                    base=0, pattern=[[1, P]], channel_multiplier=-1))
            link(pool.memset(fold[:, :], 0.0))
            for off in (0, SLOTS):
                link(pool.affine_select(out=fold[:, :], in_=fold[:, :], compare_op=ALU.not_equal, fill=1.0,
                                        base=-off, pattern=[[-1, SLOTS]], channel_multiplier=1))
            link(pool.iota(slot1[:, :, :], pattern=[[SLOTS, BLOCKS], [0, 2], [1, SLOTS]], base=1,
                           channel_multiplier=0, allow_small_or_imprecise_dtypes=True))
            link(pool.iota(block_c[:, :], pattern=[[SLOTS, BLOCKS - 1]], base=SLOTS,
                           channel_multiplier=0, allow_small_or_imprecise_dtypes=True))
            link(pool.iota(boff_c[:, :], pattern=[[P, BLOCKS - 1]], base=P,
                           channel_multiplier=0, allow_small_or_imprecise_dtypes=True))
            link(pool.iota(exp_c[:, :], pattern=[[0, 1]], base=0,
                           channel_multiplier=1, allow_small_or_imprecise_dtypes=True))
            link(pool.iota(extra1[:, :], pattern=[[1, EXTRA]], base=1,
                           channel_multiplier=0, allow_small_or_imprecise_dtypes=True))
            link(pool.memset(table_f[:, :], 0.0))
            pool.iota(table_f[:, 0:E], pattern=[[1, E]], base=0,
                      channel_multiplier=0, allow_small_or_imprecise_dtypes=True).then_inc(s_const, 1)
            for t in range(TT):
                pool.wait_ge(s_sck, 2 * (t + 1))
                pool.affine_select(out=sc[:, t, :, :], in_=sc[:, t, :, :], compare_op=ALU.is_ge, fill=0.0,
                                   base=0, pattern=[[0, HEADS], [1, P]], channel_multiplier=-1).then_inc(s_mask, 1)

        @block.scalar
        def _(act_e):
            act_e.preload_act_table_set("natural_log_exp_and_others")
            act_e.dma_start(gmix_row[:, :], norm_mix_g[0].rearrange("(a p) -> a p", p=P)).then_inc(s_gmix, 16)
            act_e.dma_start(wgk[:, :, :], win_v[:, :, GKLOW0:GKLOW0 + RANK]).then_inc(s_small, 16)
            act_e.wait_ge(s_const, 1)

            def square_sum(t, junk):
                act_e.activation(junk, xs[:, t, :], ACT.Square, accum_out=ss[:, t:t + 1]).then_inc(s_ss, 1)

            def rsqrt(norm, t):
                n = norm * TT + t
                act_e.wait_ge(s_var, n + 1)
                act_e.activation(lnv[:, t:t + 1], var[:, t:t + 1], ACT.Ln).then_inc(s_lv, 1)
                act_e.wait_ge(s_lv, n + 1)
                act_e.activation(rstd[:, t:t + 1], lnv[:, t:t + 1], ACT.Exp, scale=-0.5).then_inc(s_rs, 1)

            for t in range(TT):
                act_e.wait_ge(s_x[t], 16)
                square_sum(t, h_row[:, t, :])
            for t in range(TT):
                rsqrt(0, t)
            act_e.wait_ge(s_cols, 1)
            for i in (0, 2):
                act_e.wait_ge(s_tr, i + 1)
                for k in range(2 * i, 2 * i + 2):
                    c = slice((k % 2) * T, (k % 2 + 1) * T)
                    ins = act_e.activation(h_t[:, k, :], bank[i][:, c], ACT.Copy, scale=gmix_c[:, k:k + 1])
                ins.then_inc(s_trA, 1)
            act_e.dma_start(gffn_bc[:, :], norm_ffn_g.partition_broadcast(P)[:, 0, :]).then_inc(s_late, 16)
            act_e.dma_start(wr[:, :, :], wr_v).then_inc(s_late, 16)
            act_e.dma_start(br_bc[:, :], b_router.partition_broadcast(P)[:, 0, :]).then_inc(s_late, 16)
            act_e.dma_start(g_bc[:, :], norm_final_g.rearrange("(a d) -> a d", a=1).partition_broadcast(P)[:, 0, :]).then_inc(s_gfin, 16)

            def keep(n):
                what, i = PROJ[n]
                src = bank[n % 4]
                two = src[:, :].rearrange("p (a t) -> p a t", a=2)
                act_e.wait_ge(s_pj, n + 1)
                if what == "gk":
                    o, src_ap = gkl[:, :], src[0:RANK, 0:T]
                elif what == VV:
                    o, src_ap = v_row[:, i, :], src[:, :]
                elif what == QK:
                    o, src_ap = qk[:, i, :, :], two
                else:
                    o, src_ap = {GG: g_t, UU: u_t}[what][:, 2 * i:2 * i + 2, :], two
                act_e.copy(o, src_ap).then_inc(s_pk, 1)

            for n in range(3):
                keep(n)
            act_e.wait_ge(s_gkb, 1)
            act_e.activation(la[:, :, :], gk[:, :, :], ACT.Abs).then_inc(s_sp, 1)
            act_e.wait_ge(s_sp, 1)
            act_e.activation(lb[:, :, :], la[:, :, :], ACT.Exp, scale=-1.0).then_inc(s_sp, 1)
            act_e.wait_ge(s_sp, 2)
            act_e.activation(la[:, :, :], lb[:, :, :], ACT.Ln, bias=one_c[:, 0:1]).then_inc(s_ln, 1)
            keep(3)
            act_e.wait_ge(s_cs, 1)
            act_e.activation(e_pos[:, :, :], lb[:, :, :], ACT.Exp, scale=1.0 / NORMALIZER).then_inc(s_ex, 1)
            act_e.activation(e_neg[:, :, :], lb[:, :, :], ACT.Exp, scale=-1.0 / NORMALIZER).then_inc(s_ex, 1)
            act_e.activation(e_rem[:, :, :], gk[:, :, :], ACT.Exp, scale=1.0 / NORMALIZER).then_inc(s_ex, 1)
            for n in range(4, 7):
                keep(n)
            act_e.wait_ge(s_pk, 7)
            act_e.activation(sil[:, :, :], g_t[:, :, :], ACT.Exp, scale=-1.0).then_inc(s_sg, 1)
            for n in range(7, 9):
                keep(n)
            for i in range(2):
                act_e.wait_ge(s_o, i + 1)
                act_e.activation(o_sq[:, 2 * i:2 * i + 2, :], bank[(7, 4)[i]][:, :].rearrange("p (a t) -> p a t", a=2),
                                 ACT.Square).then_inc(s_osq, 1)
            for i in range(2):
                act_e.wait_ge(s_ms, i + 1)
                o = o_r[:, 2 * i:2 * i + 2, :]
                act_e.activation(o, bank[5 + i][:, :].rearrange("p (a t) -> p a t", a=2), ACT.Ln,
                                 scale=1.0 / DV, bias=eps_c[:, 0:1]).then_inc(s_ol, 1)
                act_e.wait_ge(s_ol, i + 1)
                act_e.activation(o, o, ACT.Exp, scale=-0.5).then_inc(s_or, 1)
            act_e.wait_ge(s_yconv, 2)
            act_e.wait_ge(s_wr, 1)
            act_e.dma_start(bgu[:, :], b_gate_up[0]).then_inc(s_bias, 16)
            for i in range(SPLITS):
                act_e.dma_start(bdn[i * E:(i + 1) * E, :], b_down[0]).then_inc(s_bias, 16)
            for t in range(TT):
                act_e.wait_ge(s_x2, 2 * (t + 1))
                if t == 0:
                    square_sum(t, h_t[:, :, P:T])
                else:
                    act_e.wait_ge(s_op, 4)
                    square_sum(t, h_row[:, t, :])
                if t == 0:
                    rsqrt(1, t)
                for i in (0, 1):
                    act_e.wait_ge(s_tr, 4 + 2 * t + i + 1)
                    act_e.copy(h_t[:, 4 * i:4 * i + 4, t * P:(t + 1) * P],
                               bank[(0, 3)[i]][:, :].rearrange("p (a t) -> p a t", a=4)).then_inc(s_trA, 1)
                if t == 0:
                    act_e.wait_ge(s_bias, 16 * (1 + SPLITS))
                    act_e.copy(bdn_sp[:, :], bdn[:, :]).then_inc(s_bh, 1)
                else:
                    rsqrt(1, t)
            act_e.wait_ge(s_lgk, 1)
            act_e.activation(ex[:, :, :], ex[:, :, :], ACT.Exp).then_inc(s_le, 1)

            act_e.preload_act_table_set("sigmoid_and_others")
            act_e.wait_ge(s_bt, 1)
            act_e.copy(bias_t[:, :, :, :].rearrange("p a f e -> p (a f e)"), bank[2][:, :]).then_inc(s_btk, 1)

            def keep_gathered(it):
                act_e.wait_ge(s_xg, it + 1)
                act_e.copy(x_sp[:, :, 0, :], bank[3][:, :].rearrange("p (k s) -> p k s", k=KT)).then_inc(s_xh, 1)


            def hi(it, u):
                i = SPLIT.index(u)
                j = u // 4
                act_e.wait_ge(s_slot[item_slot(j)], item_loaded(it, j))
                v = SPLIT[i - BUFS]
                back = 0 if i >= BUFS else 1
                if v % 4 == 3:
                    act_e.wait_ge(s_used, it * ITEM_CHUNKS + (MIX_CHUNKS + v // 4 + 1 - back * ITEM_CHUNKS))
                else:
                    act_e.wait_ge(s_free, it * len(FREED) + (AHEAD + FREED.index(v) + 1 - back * len(FREED)))
                act_e.copy(w_hi[:, i % BUFS, :], ring[:, item_slot(j), (u % 4) * UNIT:(u % 4 + 1) * UNIT]).then_inc(s_hi, 1)

            def high_parts(it, last):
                def keep_up(c):
                    act_e.wait_ge(s_used, it * ITEM_CHUNKS + (MIX_CHUNKS + c + 1))
                    act_e.wait_ge(s_gu, it * 4 + (c + 1))
                    act_e.copy(up_sb[:, c % 2, :], bank[c % 2][:, :]).then_inc(s_up, 1)

                def sigmoid(h):
                    act_e.wait_ge(s_gl, it * 2 + (h + 1))
                    act_e.activation(g_sig[:, :, :], g_lim[:, :, :], ACT.Sigmoid, scale=ALPHA).then_inc(s_sig, 1)

                def act_high(h):
                    act_e.wait_ge(s_av, it * 2 + (h + 1))
                    act_e.copy(a_sp[:, 4 * h:4 * h + 4, 0, :], act[:, :, :]).then_inc(s_ah, 1)

                for u in (4, 5, 6):
                    hi(it, u)
                keep_up(0)
                hi(it, 8)
                act_e.wait_ge(s_pt, it + 1)
                act_e.copy(p_t[:, :], bank[3][:, 0:T])
                act_e.copy(gate_s[:, :], bank[3][:, T:T + 1]).then_inc(s_ptk, 1)
                for u in (9, 10, 11):
                    hi(it, u)
                keep_up(1)
                for u in (13, 14, 15):
                    hi(it, u)
                sigmoid(0)
                keep_up(2)
                hi(it, 17)
                act_high(0)
                hi(it, 19)
                hi(it, 20)
                keep_up(3)
                hi(it, 21)
                sigmoid(1)
                hi(it, 22)
                act_high(1)
                hi(it, 23)
                if not last:
                    for u in SPLIT[:BUFS - 1]:
                        hi(it + 1, u)
                for i, nn in enumerate((1, 0)):
                    if i == 0:
                        act_e.wait_ge(s_dn, it + 1)
                        act_e.wait_ge(s_ptk, it + 1)
                    else:
                        act_e.wait_ge(s_used, it * ITEM_CHUNKS + (MIX_CHUNKS + ITEM_CHUNKS))
                    act_e.activation(z_hi[:, nn * 512:(nn + 1) * 512], bank[nn][:, :], ACT.Copy,
                                     scale=gate_s[:, 0:1]).then_inc(s_zh, 1)
                if not last:
                    hi(it + 1, SPLIT[BUFS - 1])
                    keep_gathered(it + 1)

            act_e.wait_ge(s_lg, 1)
            for u in SPLIT[:BUFS]:
                hi(0, u)
            keep_gathered(0)
            act_e.wait_ge(s_mixed, 2)
            act_e.wait_ge(s_items, 2)
            final = act_e.value_load(n_items[0:1, 1:2], min_val=E - 1, max_val=E + EXTRA - 1)
            with act_e.Fori(0, final) as it:
                high_parts(it, last=False)
            high_parts(final, last=True)

            act_e.preload_act_table_set("natural_log_exp_and_others")
            for t in range(TT):
                act_e.wait_ge(s_x3, TT + t + 1)
                square_sum(t, y_out[:, t, :])
                rsqrt(2, t)

        @block.vector
        def _(dve):
            steps = [0]

            def link(ins):
                steps[0] += 1
                ins.then_inc(s_dve, 1)
                dve.wait_ge(s_dve, steps[0])

            def rstd_of(norm, t):
                n = norm * TT + t
                c = slice(t, t + 1)
                dve.wait_ge(s_ss, n + 1)
                dve.tensor_scalar(var[:, c], ss[:, c], 1.0 / D, EPS, ALU.mult, ALU.add).then_inc(s_var, 1)
                dve.wait_ge(s_rs, n + 1)
                dve.tensor_tensor(tmp2[:, c], rstd[:, c], rstd[:, c], ALU.mult).then_inc(s_rr, 1)
                dve.wait_ge(s_rr, 4 * n + 1)
                dve.tensor_tensor(tmp2[:, c], tmp2[:, c], var[:, c], ALU.mult).then_inc(s_rr, 1)
                dve.wait_ge(s_rr, 4 * n + 2)
                dve.tensor_scalar(tmp2[:, c], tmp2[:, c], -0.5, 1.5, ALU.mult, ALU.add).then_inc(s_rr, 1)
                dve.wait_ge(s_rr, 4 * n + 3)
                dve.tensor_tensor(rstd[:, c], rstd[:, c], tmp2[:, c], ALU.mult).then_inc(s_rr, 1)
                dve.wait_ge(s_rr, 4 * n + 4)

            dve.wait_ge(s_small_t, 1)
            dve.tensor_copy(gmix_c[:, :], bank[4][:, 0:KT]).then_inc(s_cols, 1)
            for t in range(TT):
                rstd_of(0, t)
                dve.tensor_scalar(h_row[:, t, :], xs[:, t, :], rstd[:, t:t + 1], None, ALU.mult).then_inc(s_h, 1)
            dve.wait_ge(s_cols, 1)
            for i in (1, 3):
                dve.wait_ge(s_tr, i + 1)
                for k in range(2 * i, 2 * i + 2):
                    c = slice((k % 2) * T, (k % 2 + 1) * T)
                    ins = dve.tensor_scalar(h_t[:, k, :], bank[i][:, c], gmix_c[:, k:k + 1], None, ALU.mult)
                ins.then_inc(s_trD, 1)
            dve.wait_ge(s_small_t, 2)
            dve.tensor_copy(cols[:, :], bank[4][:, 0:NCOLS]).then_inc(s_cols, 1)

            dve.wait_ge(s_gk, 1)
            dve.wait_ge(s_cols, 2)
            for a in range(PAIRS):
                ins = dve.tensor_scalar(gk[:, a, :], bank[4][:, a * T:(a + 1) * T], cols[:, a:a + 1], None, ALU.add)
            ins.then_inc(s_gkb, 1)
            dve.wait_ge(s_const, 2)
            dve.wait_ge(s_ln, 1)
            link(dve.scalar_tensor_tensor(out=lb[:, :, :], in0=gk[:, :, :], scalar=0.0, in1=la[:, :, :],
                                          op0=ALU.min, op1=ALU.subtract))
            link(dve.tensor_copy(la[:, :, :], lb[:, :, :]))
            link(dve.tensor_tensor_scan(out=lb[:, :, :].rearrange("p a t -> p (a t)"),
                                        data0=reset[:, :, :].rearrange("p a t -> p (a t)"),
                                        data1=la[:, :, :].rearrange("p a t -> p (a t)"),
                                        initial=0.0, op0=ALU.mult, op1=ALU.add))
            lb_c = lb[:, :, :].rearrange("p a (n c) -> p (a n) c", c=CH)
            gk_c = gk[:, :, :].rearrange("p a (n c) -> p (a n) c", c=CH)
            dve.tensor_tensor(gk_c, lb_c[:, :, CH - 1:CH].broadcast_to([P, PAIRS * NCH, CH]), lb_c,
                              ALU.subtract).then_inc(s_cs, 1)
            dve.wait_ge(s_pk, 2)
            dve.wait_ge(s_ex, 1)
            dve.scalar_tensor_tensor(out=q_dec[:, :, :], in0=qk[:, 0, :, :], scalar=DK ** -0.5, in1=e_pos[:, :, :],
                                     op0=ALU.mult, op1=ALU.mult).then_inc(s_dec, 1)
            dve.wait_ge(s_ex, 2)
            for a in range(2):
                r = slice(DK * a, DK * (a + 1))
                dve.tensor_tensor(k_dec[r, :, a, :], qk[r, 1, :, :], e_neg[r, :, :], ALU.mult).then_inc(s_dec, 1)
            dve.wait_ge(s_ex, 3)
            dve.tensor_tensor(k_rem[:, :, :], qk[:, 1, :, :], e_rem[:, :, :], ALU.mult).then_inc(s_dec, 1)
            dve.wait_ge(s_kt, 1)
            dve.tensor_copy(k_row[:, :, :].rearrange("p t n -> p (t n)"), bank[5][:, :]).then_inc(s_krow, 1)

            def keep_scores(t):
                dve.wait_ge(s_sc, t + 1)
                src = bank[5 + t][:, :].rearrange("p (h c) -> p h c", h=HEADS)
                for a in range(2):
                    r = slice(CH * a, CH * (a + 1))
                    dve.tensor_copy(sc[r, t, :, r], src[r, :, r]).then_inc(s_sck, 1)

            for n in range(NCH - 1):
                dve.wait_ge(s_kv, n + 1)
                kv = bank[(6, 7, 4)[n]][:, :].rearrange("p (a b v) -> p a b v", a=PAIRS, b=2)
                for b in range(2):
                    r = slice(DK * b, DK * (b + 1))
                    if n == 0:
                        ins = dve.tensor_copy(state[r, 0, :, b, :], kv[r, :, b, :])
                    else:
                        for a in range(PAIRS):
                            last = (n + 1) * CH - 1
                            ins = dve.scalar_tensor_tensor(out=state[r, n, a, b, :], in0=state[r, n - 1, a, b, :],
                                                           scalar=e_pos[r, a, last:last + 1], in1=kv[r, a, b, :],
                                                           op0=ALU.mult, op1=ALU.add)
                ins.then_inc(s_st, 1)
                dve.wait_ge(s_st, n + 1)
            keep_scores(0)
            keep_scores(1)
            dve.wait_ge(s_sg, 1)
            link(dve.tensor_scalar(sil[:, :, :], sil[:, :, :], 1.0, None, ALU.add))
            link(dve.reciprocal(sil[:, :, :], sil[:, :, :]))
            link(dve.tensor_tensor(sil[:, :, :], sil[:, :, :], g_t[:, :, :], ALU.mult))
            link(dve.tensor_scalar(sil[:, :, :], sil[:, :, :], cols[:, 2:3], None, ALU.mult))

            for i in range(2):
                r = slice(2 * i, 2 * i + 2)
                dve.wait_ge(s_pk, 8 + i)
                dve.wait_ge(s_pj, 10 + i)
                link(dve.tensor_tensor(u_pad[:, r, TAPS - 1:], two_tiles(9 + i), u_t[:, r, :], ALU.mult))
                for j in range(TAPS):
                    for c in range(2 * i, 2 * i + 2):
                        w = cols[:, 3 + j * CT + c:4 + j * CT + c]
                        src = u_pad[:, c, j:j + T]
                        if j == 0:
                            ins = dve.tensor_scalar(conv[:, c, :], src, w, None, ALU.mult)
                        else:
                            ins = dve.scalar_tensor_tensor(out=conv[:, c, :], in0=src, scalar=w, in1=conv[:, c, :],
                                                           op0=ALU.mult, op1=ALU.add)
                    link(ins)
            for i in range(2):
                r = slice(2 * i, 2 * i + 2)
                dve.wait_ge(s_or, i + 1)
                link(dve.tensor_tensor(o_r[:, r, :], bank[(7, 4)[i]][:, :].rearrange("p (a t) -> p a t", a=2),
                                       o_r[:, r, :], ALU.mult))
                dve.tensor_tensor(y_t[:, CT + 2 * i:CT + 2 * i + 2, :], o_r[:, r, :], sil[:, r, :],
                                  ALU.mult).then_inc(s_ygla, 1)
            for i in range(2):
                r = slice(2 * i, 2 * i + 2)
                dve.wait_ge(s_pj, 12 + i)
                dve.tensor_tensor(y_t[:, r, :], two_tiles(11 + i), conv[:, r, :], ALU.mult).then_inc(s_yconv, 1)

            dve.wait_ge(s_late, 16 * 3)
            dve.tensor_tensor(wr_g[:, :, :], wr[:, :, :],
                              cols[:, FFN0:NCOLS].rearrange("p (k a) -> p k a", a=1).broadcast_to([P, KT, E]),
                              ALU.mult).then_inc(s_wr, 1)
            for t in range(TT):
                for n in range(2):
                    dve.wait_ge(s_op, 2 * t + n + 1)
                    dve.tensor_tensor(xs[:, t, n * 512:(n + 1) * 512], xs[:, t, n * 512:(n + 1) * 512],
                                      bank[OUT_BANK[2 * t + n]][:, :], ALU.add).then_inc(s_x2, 1)
                rstd_of(1, t)
                dve.scalar_tensor_tensor(out=h2[:, t, :], in0=xs[:, t, :], scalar=rstd[:, t:t + 1],
                                         in1=gffn_bc[:, :], op0=ALU.mult, op1=ALU.mult).then_inc(s_h2, 1)
                if t == 0:
                    dve.wait_ge(s_bh, 1)
                    for i in (1, 3):
                        r = slice(i * E, (i + 1) * E)
                        dve.tensor_tensor(bdn_sp[r, :], bdn[r, :], bdn_sp[r, :], ALU.subtract).then_inc(s_bl, 1)

            dve.wait_ge(s_lg, 1)
            for t in range(TT):
                ins = dve.scalar_tensor_tensor(out=lg[:, t, :], in0=bank[4][:, t * E:(t + 1) * E], scalar=rstd[:, t:t + 1],
                                               in1=br_bc[:, :], op0=ALU.mult, op1=ALU.add)
            link(ins)
            for t in range(TT):
                ins = dve.max(out=lmax[:, t, :], in_=lg[:, t, :])
            link(ins)
            dve.tensor_tensor(ex[:, :, :], lg[:, :, :], lmax[:, :, 0:1].broadcast_to([P, TT, E]),
                              ALU.subtract).then_inc(s_lgk, 1)
            fourth = lmax[:, :, TOP - 1:TOP].broadcast_to([P, TT, E])
            dve.tensor_tensor(gt[:, :, :], lg[:, :, :], fourth, ALU.is_gt)
            link(dve.tensor_tensor(eq[:, :, :], lg[:, :, :], fourth, ALU.is_equal))
            dve.tensor_reduce(ngt[:, :], gt[:, :, :], AX.X, ALU.add)
            for t in range(TT):
                ins = dve.tensor_tensor_scan(out=cum[:, t, :], data0=ones[:, 0:E], data1=eq[:, t, :], initial=0.0,
                                             op0=ALU.mult, op1=ALU.add)
            link(ins)
            for t in range(TT):
                ins = dve.tensor_scalar(cum[:, t, :], cum[:, t, :], ngt[:, t:t + 1], float(TOP), ALU.add, ALU.is_le)
            link(ins)
            link(dve.tensor_tensor(eq[:, :, :], eq[:, :, :], cum[:, :, :], ALU.mult))
            dve.tensor_tensor(chosen[:, :, :], eq[:, :, :], gt[:, :, :], ALU.add).then_inc(s_cho, 1)
            dve.wait_ge(s_cnt, 1)
            link(dve.tensor_copy(cnt[:, :], bank[5][0:E, 2 * E:2 * E + 1]))
            dve.tensor_scalar(more[:, :], block_c[:, :], cnt[:, 0:1], None, ALU.is_lt).then_inc(s_more, 1)
            link(dve.scalar_tensor_tensor(out=rank1[:, :, :], in0=bank[5][:, 0:TT * E].rearrange("p (t e) -> p t e", t=TT),
                                          scalar=1.0, in1=chosen[:, :, :], op0=ALU.add, op1=ALU.mult))
            dve.wait_ge(s_le, 1)
            link(dve.tensor_tensor(ex[:, :, :], ex[:, :, :], chosen[:, :, :], ALU.mult))
            link(dve.tensor_reduce(ngt[:, :], ex[:, :, :], AX.X, ALU.add))
            link(dve.reciprocal(ngt[:, :], ngt[:, :]))
            dve.tensor_tensor(gates[:, :, :], ex[:, :, :],
                              ngt[:, :].rearrange("p (t a) -> p t a", a=1).broadcast_to([P, TT, E]), ALU.mult).then_inc(s_gtk, 1)
            dve.wait_ge(s_gtk, 1)

            def lo(it, u):
                i = SPLIT.index(u)
                dve.wait_ge(s_hi, it * len(SPLIT) + (i + 1))
                dve.tensor_tensor(w_lo[:, i % BUFS, :], ring[:, item_slot(u // 4), (u % 4) * UNIT:(u % 4 + 1) * UNIT],
                                  w_hi[:, i % BUFS, :], ALU.subtract).then_inc(s_lo, 1)

            def place_slots(e, boff):
                for t in range(TT):
                    dve.tensor_scalar(p_row[:, t, :], slot1[:, :, :].rearrange("p b s -> p (b s)")[:, ds(boff, P)],
                                      rank1[:, t, ds(e, 1)], None, ALU.is_equal)
                dve.tensor_copy(gate_c[:, :], gates[:, :, ds(e, 1)].rearrange("p t e -> p (t e)")).then_inc(s_p, 1)

            def pick_bias(e):
                dve.tensor_copy(bias_e[:, :, :], bias_t[:, :, :, ds(e, 1)].rearrange("p a f e -> p a (f e)")).then_inc(s_be, 1)

            def low_gathered(it):
                dve.wait_ge(s_xh, it + 1)
                dve.tensor_tensor(x_sp[:, :, 1, :], bank[3][:, :].rearrange("p (k s) -> p k s", k=KT),
                                  x_sp[:, :, 0, :], ALU.subtract).then_inc(s_xs, 1)

            dve.wait_ge(s_const, 3)
            place_slots(0, 0)
            dve.tensor_copy(gates4[:, :, :, :], gates[:, :, :].rearrange("p t (a e) -> p t a e", a=1)
                            .broadcast_to([P, TT, SPLITS, E])).then_inc(s_gtk, 1)
            dve.wait_ge(s_pref, 1)
            link(dve.tensor_reduce(n_f[0:1, 0:1], bank[7][0:1, 64:64 + BLOCKS - 1], AX.X, ALU.add))
            dve.tensor_scalar(n_items[0:1, 0:1], n_f[0:1, 0:1], float(E), None, ALU.add).then_inc(s_items, 1)
            dve.tensor_scalar(n_items[0:1, 1:2], n_f[0:1, 0:1], float(E - 1), None, ALU.add).then_inc(s_items, 1)
            link(dve.tensor_copy(place[:, :], bank[7][0:E, 0:BLOCKS - 1]))
            tot = BLOCKS - 1
            for b in range(1, BLOCKS - 1):
                for a in range(b):
                    link(dve.tensor_tensor(place[:, b:b + 1], place[:, b:b + 1], bank[7][0:E, tot + a:tot + a + 1], ALU.add))
            link(dve.scalar_tensor_tensor(out=place[:, :], in0=place[:, :], scalar=1.0, in1=more[:, :],
                                          op0=ALU.add, op1=ALU.mult))
            for b in range(BLOCKS - 1):
                ins = dve.tensor_scalar(hot[:, b, :], extra1[:, :], place[:, b:b + 1], None, ALU.is_equal)
            ins.then_inc(s_hot, 1)
            dve.wait_ge(s_gt, 1)
            gates_ps = bank[6][:, 0:T].rearrange("e (t p) -> e t p", t=TT)
            link(dve.tensor_copy(gates_t[:, :, :], gates_ps))
            r = slice(2 * E, P)
            dve.tensor_tensor(gates_t[r, :, :], gates_ps[r, :, :], gates_t[r, :, :], ALU.subtract).then_inc(s_gtk, 1)
            lo(0, SPLIT[0])
            dve.wait_ge(s_items, 2)
            final = dve.value_load(n_items[0:1, 1:2], min_val=E - 1, max_val=E + EXTRA - 1)
            dve.wait_ge(s_tab, 1)
            for a in range(2):
                link(dve.tensor_copy(table_f[0:1, a * TABLE + E:a * TABLE + E + EXTRA], bank[1][0:1, a * EXTRA:(a + 1) * EXTRA]))
            dve.tensor_copy(table[0:1, :], table_f[0:1, :]).then_inc(s_table, 1)
            low_gathered(0)
            dve.wait_ge(s_table, 1)

            dve.sem_inc(s_mixed, 1)
            dve.wait_ge(s_btk, 1)
            pick_bias(0)
            dve.wait_ge(s_mixed, 2)
            dve.sem_inc(s_gur, 1)

            def low_parts(it, last):
                def biased(h):
                    dve.wait_ge(s_gu, it * 4 + (2 + 2 * h + 2))
                    if h == 0:
                        dve.wait_ge(s_be, it + 1)
                    dve.tensor_tensor(gu_b[:, :, :, :],
                                      bank[2][:, :].rearrange("p (a f s) -> p a f s", a=2, f=4),
                                      bias_e[:, :, 4 * h:4 * h + 4].rearrange("p a (f s) -> p a f s", s=1)
                                      .broadcast_to([P, 2, 4, SLOTS]), ALU.add).then_inc(s_gur, 1)

                def limited(h):
                    dve.wait_ge(s_gur, it * 2 + (h + 2))
                    dve.tensor_scalar(g_lim[:, :, :], gu_b[:, 0, :, :], LIMIT, None, ALU.min).then_inc(s_gl, 1)
                    dve.tensor_scalar(u_lim[:, :, :], gu_b[:, 1, :, :], LIMIT, -LIMIT, ALU.min, ALU.max).then_inc(s_ul, 1)

                def multiplied(h):
                    dve.wait_ge(s_ul, it * 2 + (h + 1))
                    dve.wait_ge(s_gl, it * 2 + (h + 1))
                    dve.scalar_tensor_tensor(out=u_lim[:, :, :], in0=u_lim[:, :, :], scalar=1.0,
                                             in1=g_lim[:, :, :], op0=ALU.add, op1=ALU.mult).then_inc(s_um, 1)

                def activated(h):
                    dve.wait_ge(s_sig, it * 2 + (h + 1))
                    dve.wait_ge(s_um, it * 2 + (h + 1))
                    dve.tensor_tensor(act[:, :, :], g_sig[:, :, :], u_lim[:, :, :], ALU.mult).then_inc(s_av, 1)

                def low_activated(h):
                    dve.wait_ge(s_ah, it * 2 + (h + 1))
                    dve.tensor_tensor(a_sp[:, 4 * h:4 * h + 4, 1, :], act[:, :, :], a_sp[:, 4 * h:4 * h + 4, 0, :],
                                      ALU.subtract).then_inc(s_a, 1)

                for u in (4, 5, 6, 8, 9):
                    lo(it, u)
                if not last:
                    dve.wait_ge(s_pt, it + 1)
                    e_next = dve.value_load(table[0:1, ds(it + 1, 1)], min_val=0, max_val=E - 1)
                    b_next = dve.value_load(table[0:1, ds(it + (TABLE + 1), 1)], min_val=0, max_val=(BLOCKS - 1) * P)
                    place_slots(e_next, b_next)
                for u in (10, 11, 13, 14):
                    lo(it, u)
                biased(0)
                limited(0)
                multiplied(0)
                lo(it, 15)
                activated(0)
                lo(it, 17)
                low_activated(0)
                for u in (19, 20, 21):
                    lo(it, u)
                biased(1)
                limited(1)
                multiplied(1)
                activated(1)
                low_activated(1)
                lo(it, 22)
                lo(it, 23)
                if not last:
                    pick_bias(e_next)
                    for u in SPLIT[:BUFS - 1]:
                        lo(it + 1, u)
                for i, nn in enumerate((1, 0)):
                    dve.wait_ge(s_zh, it * 2 + (i + 1))
                    dve.scalar_tensor_tensor(out=z_lo[:, nn * 512:(nn + 1) * 512], in0=bank[nn][:, :],
                                             scalar=gate_s[:, 0:1], in1=z_hi[:, nn * 512:(nn + 1) * 512],
                                             op0=ALU.mult, op1=ALU.subtract).then_inc(s_zl, 1)
                if not last:
                    lo(it + 1, SPLIT[BUFS - 1])
                    low_gathered(it + 1)

            for u in SPLIT[1:BUFS]:
                lo(0, u)
            with dve.Fori(0, final) as it:
                low_parts(it, last=False)
            low_parts(final, last=True)

            for i, nn in enumerate((1, 0)):
                for t in range(TT):
                    dve.wait_ge(s_y, final + (i * TT + t + 1))
                    c = slice(nn * 512, (nn + 1) * 512)
                    dve.tensor_tensor(xs[:, t, c], xs[:, t, c], y_ps[t][nn][:, :], ALU.add).then_inc(s_x3, 1)
            for t in range(TT):
                rstd_of(2, t)
                if t == 0:
                    dve.wait_ge(s_gfin, 16)
                dve.scalar_tensor_tensor(out=y_out[:, t, :], in0=xs[:, t, :], scalar=rstd[:, t:t + 1],
                                         in1=g_bc[:, :], op0=ALU.mult, op1=ALU.mult).then_inc(s_fin, 1)

        @block.tensor
        def _(pe):
            mm = nc.tensor.matmul

            pe.wait_ge(s_const, 1)
            pe.wait_ge(s_gmix, 16)
            nc.tensor.transpose(bank[4][:, 0:KT], gmix_row[:, :], ident[0:KT, 0:KT]).then_inc(s_small_t, 1)

            for t in range(TT):
                pe.wait_ge(s_h, t + 1)
                for k in range(KT):
                    ins = nc.tensor.transpose(bank[k // 2][:, (k % 2) * T + t * P:(k % 2) * T + (t + 1) * P],
                                              h_row[:, t, k * P:(k + 1) * P], ident[:, :])
                    if t == TT - 1 and k % 2 == 1:
                        ins.then_inc(s_tr, 1)
            pe.wait_ge(s_trA, 2)
            pe.wait_ge(s_trD, 2)

            def project(n):
                what, i = PROJ[n]
                dst = bank[n % 4]
                if n >= 4:
                    pe.wait_ge(s_pk, n - 3)
                if what == "gk":
                    for k in range(KT):
                        ins = mm(dst[0:RANK, 0:T], wgk[:, k, :], h_t[:, k, :], start=k == 0, stop=k == KT - 1)
                    ins.then_inc(s_pj, 1)
                    return
                if i == 0:
                    pe.wait_ge(s_slot[slot_of(what)], 16)
                w = chunk_view(what, KT)
                if what == VV:
                    for k in range(KT):
                        ins = mm(dst[:, :], h_t[:, k, i * P:(i + 1) * P], w[:, k, :], start=k == 0, stop=k == KT - 1)
                else:
                    for m in range(2):
                        for k in range(KT):
                            ins = mm(dst[:, m * T:(m + 1) * T], w[:, k, (2 * i + m) * P:(2 * i + m + 1) * P],
                                     h_t[:, k, :], start=k == 0, stop=k == KT - 1)
                ins.then_inc(s_pj, 1)
                if i == 1:
                    pe.wait_ge(s_pj, n + 1)
                    pe.sem_inc(s_used, 1)

            project(0)
            pe.wait_ge(s_small, 16 * 8)
            pe.wait_ge(s_cols, 1)
            nc.tensor.transpose(bank[4][:, 0:NCOLS], rows[:, :], ident[0:NCOLS, 0:NCOLS]).then_inc(s_small_t, 1)
            project(1)
            project(2)
            pe.wait_ge(s_pk, 3)
            pe.wait_ge(s_cols, 2)
            for a in range(PAIRS):
                ins = mm(bank[4][:, a * T:(a + 1) * T], wgu[:, a, :], gkl[:, :], start=True, stop=True)
            ins.then_inc(s_gk, 1)
            project(3)
            project(4)
            pe.wait_ge(s_dec, 4)
            for t in range(TT):
                for a in range(PAIRS):
                    ins = nc.tensor.transpose(bank[5][:, (t * PAIRS + a) * P:(t * PAIRS + a + 1) * P],
                                              k_rem[:, a, t * P:(t + 1) * P], ident[:, :])
            ins.then_inc(s_kt, 1)
            project(5)
            project(6)
            pe.wait_ge(s_krow, 1)
            pe.wait_ge(s_pk, 5)
            for n in range(NCH - 1):
                r = slice(CH * (n % 2), CH * (n % 2 + 1))
                for a in range(PAIRS):
                    ins = mm(bank[(6, 7, 4)[n]][:, a * 2 * DV:(a + 1) * 2 * DV], k_row[r, n // 2, a * P:(a + 1) * P],
                             v_row[r, n // 2, a * 2 * DV:(a + 1) * 2 * DV], start=True, stop=True)
                ins.then_inc(s_kv, 1)
            for t in range(TT):
                if t == 1:
                    pe.wait_ge(s_st, 1)
                for h in range(HEADS):
                    ins = mm(bank[5 + t][:, h * P:(h + 1) * P], k_dec[:, h // 2, h % 2, t * P:(t + 1) * P],
                             q_dec[:, h // 2, t * P:(t + 1) * P], start=True, stop=True)
                ins.then_inc(s_sc, 1)
            project(7)
            project(8)
            pe.wait_ge(s_mask, 2)
            pe.wait_ge(s_st, 3)
            for i in range(2):
                dst = bank[(7, 4)[i]]
                for h in range(2 * i, 2 * i + 2):
                    for t in range(TT):
                        c0 = (h % 2) * T + t * P
                        mm(dst[:, c0:c0 + P], v_row[:, t, h * DV:(h + 1) * DV], sc[:, t, h, :], start=True, stop=False)
                        for n in range(2 * t, 2 * t + 2):
                            if n == 0:
                                continue
                            c1 = c0 + CH * (n % 2)
                            ins = mm(dst[:, c1:c1 + CH], state[:, n - 1, h // 2, h % 2, :],
                                     q_dec[:, h // 2, n * CH:(n + 1) * CH], start=False, stop=n % 2 == 1)
                ins.then_inc(s_o, 1)
            project(9)
            project(10)
            for i in range(2):
                pe.wait_ge(s_osq, i + 1)
                pe.wait_ge(s_sck, 2 * (i + 1))
                mm(bank[5 + i][:, :], ones[:, :], o_sq[:, 2 * i:2 * i + 2, :].rearrange("p a t -> p (a t)"),
                   start=True, stop=True).then_inc(s_ms, 1)
            project(11)
            project(12)
            pe.wait_ge(s_ygla, 2)
            def out_project(t, n):
                w = chunk_view(WO + n, KT)
                if t == 0:
                    pe.wait_ge(s_slot[slot_of(WO + n)], 32)
                for j, k in enumerate(list(range(CT, KT)) + list(range(CT))):
                    if t == 0 and n == 0 and k in (0, 2):
                        pe.wait_ge(s_yconv, k // 2 + 1)
                    ins = mm(bank[OUT_BANK[2 * t + n]][:, :], y_t[:, k, t * P:(t + 1) * P], w[:, k, :],
                             start=j == 0, stop=j == KT - 1)
                ins.then_inc(s_op, 1)

            def transpose_x(t):
                pe.wait_ge(s_x2, 2 * (t + 1))
                pe.wait_ge(s_trA, 2 + 2 * t)
                for i in range(2):
                    for k in range(4):
                        ins = nc.tensor.transpose(bank[(0, 3)[i]][:, k * P:(k + 1) * P],
                                                  xs[:, t, (4 * i + k) * P:(4 * i + k + 1) * P], ident[:, :])
                    ins.then_inc(s_tr, 1)

            def logits(t):
                pe.wait_ge(s_trA, 2 + 2 * (t + 1))
                for k in range(KT):
                    ins = mm(bank[4][:, t * E:(t + 1) * E], h_t[:, k, t * P:(t + 1) * P], wr_g[:, k, :],
                             start=k == 0, stop=k == KT - 1)
                return ins

            out_project(0, 0)
            out_project(0, 1)
            out_project(1, 0)
            transpose_x(0)
            out_project(1, 1)
            pe.wait_ge(s_wr, 1)
            logits(0)
            pe.wait_ge(s_op, 4)
            pe.sem_inc(s_used, 2)
            transpose_x(1)
            logits(1).then_inc(s_lg, 1)
            pe.sem_inc(s_free, AHEAD)
            pe.wait_ge(s_bias, 16 * (1 + SPLITS))
            for i in range(2 * F // P):
                ins = nc.tensor.transpose(bank[2][:, i * E:(i + 1) * E], bgu[:, i * P:(i + 1) * P], ident[0:E, 0:E])
            ins.then_inc(s_bt, 1)
            pe.wait_ge(s_cho, 1)
            pe.wait_ge(s_const, 3)
            mm(bank[5][:, 0:E], before[:, :], chosen[:, 0, :], start=True, stop=True)
            mm(bank[5][:, E:2 * E], before[:, :], chosen[:, 1, :], start=True, stop=False)
            mm(bank[5][:, E:2 * E], ones[:, :], chosen[:, 0, :], start=False, stop=True)
            for t in range(TT):
                ins = mm(bank[5][0:E, 2 * E:2 * E + 1], chosen[:, t, :], ones[:, 0:1], start=t == 0, stop=t == TT - 1)
            ins.then_inc(s_cnt, 1)
            pe.wait_ge(s_more, 1)
            nb = BLOCKS - 1
            mm(bank[7][0:E, 0:nb], before[0:E, 0:E], more[:, :], start=True, stop=True)
            mm(bank[7][0:E, nb:2 * nb], ones[0:E, 0:E], more[:, :], start=True, stop=True)
            mm(bank[7][0:1, 64:64 + nb], ones[0:E, 0:1], more[:, :], start=True, stop=True).then_inc(s_pref, 1)
            pe.wait_ge(s_gtk, 2)
            for t in range(TT):
                ins = nc.tensor.transpose(bank[6][:, t * P:(t + 1) * P],
                                          gates4[:, t, :, :].rearrange("p a e -> p (a e)"), ident[:, :])
            ins.then_inc(s_gt, 1)

            def gather(tiles=range(KT)):
                for k in tiles:
                    for t in range(TT):
                        ins = mm(bank[3][:, k * SLOTS:(k + 1) * SLOTS], h2[:, t, k * P:(k + 1) * P],
                                 p_row[:, t, 0:SLOTS].bitcast(f32), start=t == 0, stop=t == TT - 1)
                if k == KT - 1:
                    ins.then_inc(s_xg, 1)

            pe.wait_ge(s_h2, 2)
            pe.wait_ge(s_p, 1)
            gather(range(KT // 2))
            pe.wait_ge(s_hot, 1)
            pe.wait_ge(s_gtk, 3)
            pe.wait_ge(s_bl, 2)
            for t in range(TT):
                for nn in range(2):
                    ins = mm(y_ps[t][nn][:, :], gates_t[:, t, :], bdn_sp[:, nn * 512:(nn + 1) * 512], start=True, stop=True)
            ins.then_inc(s_mixed, 1)
            gather(range(KT // 2, KT))
            for a in range(2):
                for b in range(nb):
                    ins = mm(bank[1][0:1, a * EXTRA:(a + 1) * EXTRA],
                             exp_c[:, 0:1] if a == 0 else boff_c[:, b:b + 1], hot[:, b, :],
                             start=b == 0, stop=b == nb - 1)
            ins.then_inc(s_tab, 1)
            pe.wait_ge(s_items, 2)
            final = pe.value_load(n_items[0:1, 1:2], min_val=E - 1, max_val=E + EXTRA - 1)
            pe.wait_ge(s_table, 1)
            pe.wait_ge(s_btk, 1)
            pe.sem_inc(s_gu, 2)

            def products(it, last):
                def unit(u, frees=False, between=None):
                    j, uu = u // 4, u % 4
                    slot = ring[:, item_slot(j), uu * UNIT:(uu + 1) * UNIT]
                    if u in WHOLE:
                        if uu == 0:
                            pe.wait_ge(s_slot[item_slot(j)], item_loaded(it, j))
                        parts = [slot]
                    else:
                        i = SPLIT.index(u)
                        pe.wait_ge(s_lo, it * len(SPLIT) + (i + 1))
                        parts = [w_hi[:, i % BUFS, :], w_lo[:, i % BUFS, :]]
                    whole = u in WHOLE

                    def stationary(ap):
                        return ap.bitcast(f32) if whole else ap

                    if j < 4:
                        for kk in range(2):
                            k = 2 * uu + kk
                            lhs = stationary(x_sp[:, k, :, :].rearrange("p a s -> p (a s)"))
                            for q, w in enumerate(parts):
                                ins = mm(bank[j % 2][:, :], lhs, w[:, kk * 512:(kk + 1) * 512],
                                         start=k == 0 and q == 0, stop=k == KT - 1 and q == len(parts) - 1)
                    else:
                        k = 4 * (j - 4) + uu
                        lhs = stationary(a_sp[:, k, :, :].rearrange("p a s -> p (a s)"))
                        for nn in (0, 1) if between else (1, 0):
                            for q, w in enumerate(parts):
                                ins = mm(bank[nn][:, :], lhs, w[:, nn * 512:(nn + 1) * 512],
                                         start=k == 0 and q == 0, stop=k == KT - 1 and q == len(parts) - 1)
                            if k == KT - 1 and nn == 1:
                                ins.then_inc(s_dn, 1)
                            if between and nn == 0:
                                between()
                    if frees:
                        ins.then_inc(s_used, 1)
                    elif not whole:
                        ins.then_inc(s_free, 1)

                def chunk(j):
                    for uu in range(4):
                        unit(4 * j + uu, frees=uu == 3)

                def fold_up(c):
                    pe.wait_ge(s_up, it * 4 + (c + 1))
                    if c % 2 == 0:
                        pe.wait_ge(s_gur, it * 2 + (c // 2 + 1))
                    for f in range(4):
                        o = (c % 2) * 4 * SLOTS + f * SLOTS
                        ins = mm(bank[2][:, o:o + SLOTS], up_sb[:, c % 2, f * P:(f + 1) * P], fold[:, :],
                                 start=True, stop=True)
                    ins.then_inc(s_gu, 1)

                pe.wait_ge(s_xs, it + 1)
                chunk(0)
                for t in range(TT):
                    nc.tensor.transpose(bank[3][:, t * P:(t + 1) * P], p_row[:, t, :].bitcast(f32), ident[:, :])
                for t in range(TT):
                    ins = mm(bank[3][:, T:T + 1], p_row[:, t, :].bitcast(f32), gate_c[:, t:t + 1],
                             start=t == 0, stop=t == TT - 1)
                ins.then_inc(s_pt, 1)
                unit(4)
                unit(5)
                fold_up(0)
                unit(6)
                unit(7, frees=True)
                unit(8)
                unit(9)
                fold_up(1)
                unit(10)
                unit(11, frees=True)
                unit(12)
                unit(13)
                fold_up(2)
                unit(14)
                unit(15, frees=True)
                pe.wait_ge(s_a, it * 2 + 1)
                unit(16, between=lambda: fold_up(3))
                unit(17)
                unit(18)
                unit(19, frees=True)
                pe.wait_ge(s_a, it * 2 + 2)
                chunk(5)
                if not last:
                    pe.wait_ge(s_p, it + 2)
                    pe.wait_ge(s_ptk, it + 1)
                    gather()
                for i, nn in enumerate((1, 0)):
                    pe.wait_ge(s_zl, it * 2 + (i + 1))
                    for t in range(TT):
                        for q, z in enumerate((z_hi, z_lo)):
                            ins = mm(y_ps[t][nn][:, :], p_t[:, t * P:(t + 1) * P], z[:, nn * 512:(nn + 1) * 512],
                                     start=False, stop=False, skip_group_check=True)
                        if last or (t, nn) == (TT - 1, 0):
                            ins.then_inc(s_y, 1)

            with pe.Fori(0, final) as it:
                products(it, last=False)
            products(final, last=True)


_INS = ["x", "norm_mix_g", "w_in", "conv_w", "w_gk_up", "b_gk_up", "gla_norm_g", "w_out", "norm_ffn_g",
        "w_router", "b_router", "w_gate_up", "b_gate_up", "w_down", "b_down", "norm_final_g"]


def kernel(**inputs):
    import numpy as _np
    import concourse.bacc as _bacc
    from concourse import mybir as _mybir
    from concourse.bass_utils import run_bass_kernel_spmd as _run

    nc = _bacc.Bacc("TRN2", target_bir_lowering=False, num_devices=1)
    arrays, args = {}, []
    for name in _INS:
        a = _np.ascontiguousarray(inputs[name])
        arrays[f"in_{name}"] = a
        args.append(nc.dram_tensor(f"in_{name}", a.shape, _mybir.dt.from_np(a.dtype), kind="ExternalInput").ap())
    args.append(nc.dram_tensor("out", (1, T, D), _mybir.dt.float32, kind="ExternalOutput").ap())
    build(nc, *args)
    r = _run(nc, [arrays], core_ids=[0])
    return r.results[0]["out"]
```
